# Optimizing a Trainium2 kernel written in Bass

```python
import jax, jax.numpy as jnp
from jax import lax
import numpy as np

D_MODEL = 1024
BATCH = 1
SEQ = 1024
DEPTH = 2
DEC_BATCH = 8
DEC_SEQ = 8
PAST_LEN = 8192
PAGE_SIZE = 128

EXPAND = 2
W_MIX = EXPAND * D_MODEL
W_A = W_MIX // 2
W_B = W_MIX // 2
W_C = W_MIX
POOL_WINDOWS = (2, 4, 8, 16)
N_POOL_GROUPS = len(POOL_WINDOWS)
POOL_GROUP = W_A // N_POOL_GROUPS
POOL_HIST = max(POOL_WINDOWS) - 1
CONV_B_WIDTH = 31
CONV_B_HIST = CONV_B_WIDTH - 1
CONV_C_WIDTH = 3
CONV_C_HIST = CONV_C_WIDTH - 1
N_MEM = 256
N_XHEADS = 4
XHEAD_DIM = D_MODEL // N_XHEADS
N_EVEN = (DEPTH + 1) // 2
N_ODD = DEPTH // 2
EPS = 1e-6

kernel_name = 'hybrid_pool_conformer_shortconv_decoder_step'

def rmsnorm(x, g):
    xf = x.astype(jnp.float32)
    y = xf * lax.rsqrt(jnp.mean(xf * xf, axis=-1, keepdims=True) + EPS)
    return (y * g.astype(jnp.float32)).astype(x.dtype)

def layernorm(x, g, b):
    xf = x.astype(jnp.float32)
    mu = jnp.mean(xf, axis=-1, keepdims=True)
    var = jnp.mean(jnp.square(xf - mu), axis=-1, keepdims=True)
    y = (xf - mu) * lax.rsqrt(var + EPS) * g.astype(jnp.float32) + b.astype(jnp.float32)
    return y.astype(x.dtype)

def causal_dwconv(u_full, w):
    C = w.shape[1]
    return lax.conv_general_dilated(u_full, w[:, None, :].astype(u_full.dtype), window_strides=(1,),
                                    padding='VALID', dimension_numbers=('NWC', 'WIO', 'NWC'),
                                    feature_group_count=C)

def multiscale_pool_minus_self(u_full, start_pos):
    Bn, L, _ = u_full.shape
    T = L - POOL_HIST
    uf = u_full.astype(jnp.float32).reshape(Bn, L, N_POOL_GROUPS, POOL_GROUP)
    cs = jnp.concatenate([jnp.zeros_like(uf[:, :1]), jnp.cumsum(uf, axis=1)], axis=1)
    hi = cs[:, POOL_HIST + 1:]
    pos = start_pos + jnp.arange(T)
    outs = []
    for g, w in enumerate(POOL_WINDOWS):
        lo = cs[:, POOL_HIST + 1 - w: POOL_HIST + 1 - w + T, g]
        cnt = jnp.minimum(pos + 1, w).astype(jnp.float32)
        outs.append((hi[:, :, g] - lo) / cnt[None, :, None])
    mean = jnp.stack(outs, axis=2)
    return (mean - uf[:, POOL_HIST:]).astype(u_full.dtype)

def even_mixer(h, hist_pool, hist_conv, start_pos, w_in, pool_w, pool_scale, conv_w, conv_b, ln_g, ln_b, w_out):
    Bn, T, _ = h.shape
    z = jnp.einsum('btd,de->bte', h, w_in)
    a_in, a_gate, b_val, b_glu, b_gate = jnp.split(z, [W_A, 2 * W_A, 2 * W_A + W_B, 2 * W_A + 2 * W_B], axis=-1)
    a_full = jnp.concatenate([hist_pool.astype(a_in.dtype), a_in], axis=1)
    a = multiscale_pool_minus_self(a_full, start_pos)
    a = jnp.einsum('btgc,gce->btge', a, pool_w).reshape(Bn, T, W_A) * pool_scale
    a = a * jax.nn.silu(a_gate)
    v = b_val * jax.nn.sigmoid(b_glu)
    v_full = jnp.concatenate([hist_conv.astype(v.dtype), v], axis=1)
    c = causal_dwconv(v_full, conv_w) + conv_b
    c = jax.nn.silu(layernorm(c, ln_g, ln_b)) * jax.nn.silu(b_gate)
    y = jnp.einsum('bte,ed->btd', jnp.concatenate([a, c], axis=-1), w_out)
    return y, a_full[:, -POOL_HIST:], v_full[:, -CONV_B_HIST:]

def odd_mixer(h, hist_short, w_in, short_w, w_out):
    z = jnp.einsum('btd,de->bte', h, w_in)
    gb, gc, xv, g = jnp.split(z, 4, axis=-1)
    u = gc * xv
    u_full = jnp.concatenate([hist_short.astype(u.dtype), u], axis=1)
    y = gb * causal_dwconv(u_full, short_w) * jax.nn.silu(g)
    return jnp.einsum('bte,ed->btd', y, w_out), u_full[:, -CONV_C_HIST:]

def mem_kv(mem, g, w_k, w_v):
    Bn = mem.shape[0]
    m = rmsnorm(mem, g)
    k = jnp.einsum('bmd,de->bme', m, w_k).reshape(Bn, N_MEM, N_XHEADS, XHEAD_DIM)
    v = jnp.einsum('bmd,de->bme', m, w_v).reshape(Bn, N_MEM, N_XHEADS, XHEAD_DIM)
    return k, v

def cross_attend(h, k, v, w_q, w_o):
    Bn, T, _ = h.shape
    q = jnp.einsum('btd,de->bte', h, w_q).reshape(Bn, T, N_XHEADS, XHEAD_DIM)
    s = jnp.einsum('bthd,bmhd->bhtm', q, k.astype(q.dtype)).astype(jnp.float32) * (XHEAD_DIM ** -0.5)
    p = jax.nn.softmax(s, axis=-1).astype(q.dtype)
    o = jnp.einsum('bhtm,bmhd->bthd', p, v.astype(q.dtype)).reshape(Bn, T, N_XHEADS * XHEAD_DIM)
    return jnp.einsum('bte,ed->btd', o, w_o)

def run_trunk(x, hist_pool, hist_conv, hist_short, mem_k, mem_v, start_pos,
              norm_mix, w_in_even, pool_w, pool_scale, conv_w, conv_b, ln_g, ln_b, w_out_even,
              w_in_odd, short_w, w_out_odd, norm_x, w_q, w_o, final_norm):
    new_pool, new_conv, new_short = [], [], []
    for l in range(DEPTH):
        h = rmsnorm(x, norm_mix[l])
        if l % 2 == 0:
            e = l // 2
            y, sp, sc = even_mixer(h, hist_pool[e], hist_conv[e], start_pos, w_in_even[e], pool_w[e], pool_scale[e],
                                   conv_w[e], conv_b[e], ln_g[e], ln_b[e], w_out_even[e])
            new_pool.append(sp)
            new_conv.append(sc)
        else:
            o = l // 2
            y, ss = odd_mixer(h, hist_short[o], w_in_odd[o], short_w[o], w_out_odd[o])
            new_short.append(ss)
        x = x + y
        x = x + cross_attend(rmsnorm(x, norm_x[l]), mem_k[l], mem_v[l], w_q[l], w_o[l])
    return rmsnorm(x, final_norm), jnp.stack(new_pool), jnp.stack(new_conv), jnp.stack(new_short)

def setup_inputs(seed: int = 0) -> dict:
    key = jax.random.key(seed)
    ks = jax.random.split(key, 32)
    f32 = jnp.float32
    nrm = lambda k, shape, s: (jax.random.normal(k, shape, f32) * s).astype(f32)
    D = D_MODEL
    return {
        'x_prompt': nrm(ks[0], (BATCH, SEQ, D), 1.0),
        'x_sample': nrm(ks[1], (DEC_BATCH, DEC_SEQ, D), 1.0),
        'state_pool': nrm(ks[2], (N_EVEN, DEC_BATCH, POOL_HIST, W_A), 1.0),
        'state_conv': nrm(ks[3], (N_EVEN, DEC_BATCH, CONV_B_HIST, W_B), 0.5),
        'state_short': nrm(ks[4], (N_ODD, DEC_BATCH, CONV_C_HIST, W_C), 1.0),
        'cache_mem_k': nrm(ks[5], (DEPTH, DEC_BATCH, N_MEM, N_XHEADS, XHEAD_DIM), 1.0),
        'cache_mem_v': nrm(ks[6], (DEPTH, DEC_BATCH, N_MEM, N_XHEADS, XHEAD_DIM), 1.0),
        'mem_prompt': nrm(ks[7], (BATCH, N_MEM, D), 1.0),
        'norm_mix': 1.0 + nrm(ks[8], (DEPTH, D), 0.02),
        'w_in_even': nrm(ks[9], (N_EVEN, D, 2 * W_A + 3 * W_B), D ** -0.5),
        'pool_w': nrm(ks[10], (N_EVEN, N_POOL_GROUPS, POOL_GROUP, POOL_GROUP), POOL_GROUP ** -0.5),
        'pool_scale': 1.0 + nrm(ks[11], (N_EVEN, W_A), 0.02),
        'conv_w': nrm(ks[12], (N_EVEN, CONV_B_WIDTH, W_B), CONV_B_WIDTH ** -0.5),
        'conv_b': nrm(ks[13], (N_EVEN, W_B), 0.02),
        'ln_g': 1.0 + nrm(ks[14], (N_EVEN, W_B), 0.02),
        'ln_b': nrm(ks[15], (N_EVEN, W_B), 0.02),
        'w_out_even': nrm(ks[16], (N_EVEN, W_A + W_B, D), (W_A + W_B) ** -0.5),
        'w_in_odd': nrm(ks[17], (N_ODD, D, 4 * W_C), D ** -0.5),
        'short_w': nrm(ks[18], (N_ODD, CONV_C_WIDTH, W_C), CONV_C_WIDTH ** -0.5),
        'w_out_odd': nrm(ks[19], (N_ODD, W_C, D), W_C ** -0.5),
        'norm_x': 1.0 + nrm(ks[20], (DEPTH, D), 0.02),
        'norm_mem': 1.0 + nrm(ks[21], (DEPTH, D), 0.02),
        'w_q': nrm(ks[22], (DEPTH, D, N_XHEADS * XHEAD_DIM), D ** -0.5),
        'w_k': nrm(ks[23], (DEPTH, D, N_XHEADS * XHEAD_DIM), D ** -0.5),
        'w_v': nrm(ks[24], (DEPTH, D, N_XHEADS * XHEAD_DIM), D ** -0.5),
        'w_o': nrm(ks[25], (DEPTH, N_XHEADS * XHEAD_DIM, D), (N_XHEADS * XHEAD_DIM) ** -0.5),
        'final_norm': 1.0 + nrm(ks[26], (D,), 0.02),
    }

def reference(x_prompt, x_sample, state_pool, state_conv, state_short, cache_mem_k, cache_mem_v, mem_prompt,
              norm_mix, w_in_even, pool_w, pool_scale, conv_w, conv_b, ln_g, ln_b, w_out_even,
              w_in_odd, short_w, w_out_odd, norm_x, norm_mem, w_q, w_k, w_v, w_o, final_norm):
    dt = x_prompt.dtype
    kv = [mem_kv(mem_prompt, norm_mem[l], w_k[l], w_v[l]) for l in range(DEPTH)]
    mem_k_p = jnp.stack([k for k, _ in kv])
    mem_v_p = jnp.stack([v for _, v in kv])
    zp = jnp.zeros((N_EVEN, BATCH, POOL_HIST, W_A), dt)
    zc = jnp.zeros((N_EVEN, BATCH, CONV_B_HIST, W_B), dt)
    zs = jnp.zeros((N_ODD, BATCH, CONV_C_HIST, W_C), dt)
    y_prompt, pool_p, conv_p, short_p = run_trunk(
        x_prompt, zp, zc, zs, mem_k_p, mem_v_p, 0,
        norm_mix, w_in_even, pool_w, pool_scale, conv_w, conv_b, ln_g, ln_b, w_out_even,
        w_in_odd, short_w, w_out_odd, norm_x, w_q, w_o, final_norm)
    y_sample, pool_s, conv_s, short_s = run_trunk(
        x_sample, state_pool, state_conv, state_short, cache_mem_k, cache_mem_v, PAST_LEN,
        norm_mix, w_in_even, pool_w, pool_scale, conv_w, conv_b, ln_g, ln_b, w_out_even,
        w_in_odd, short_w, w_out_odd, norm_x, w_q, w_o, final_norm)
    return (y_prompt, y_sample, pool_p, conv_p, short_p, mem_k_p, mem_v_p, pool_s, conv_s, short_s)


_drawn_inputs = setup_inputs


def setup_inputs(seed=0):
    import zlib

    import numpy as np

    out = dict(_drawn_inputs(seed))
    spreads = {}
    factors = {'pool_scale': 5.4,
     'conv_b': 4.241,
     'ln_g': 7.34,
     'ln_b': 8.0,
     'norm_x': 8.0,
     'norm_mem': 2.762,
     'final_norm': 2.777}
    for name, (base, spread) in spreads.items():
        noise = np.random.default_rng([zlib.crc32(name.encode()), seed]).standard_normal(out[name].shape)
        drawn = base * np.exp(spread * noise) if base else spread * noise
        out[name] = __import__('jax').numpy.asarray(drawn.astype(out[name].dtype))
    for name, factor in factors.items():
        out[name] = (out[name] * factor).astype(out[name].dtype)
    return out
```

```python
from contextlib import ExitStack

import concourse.bass as bass
from concourse import mybir

F32 = mybir.dt.float32
F32R = mybir.dt.float32r
ALU = mybir.AluOpType
ACT = mybir.ActivationFunctionType
AX_X = mybir.AxisListType.X

P = 128
D = 1024
KD = D // P
T = 1024
NB, TS = 8, 8
NS = NB * TS
TA = T + NS
PART = 364
TP = 3 * PART
WB = 1024
WC = 2048
CONV = 31
HC = CONV - 1
HPOOL = 15
HS = 2
MEM = 256
NH = 4
HD = 256
EPS = 1e-6
UNIT = 512
RAW, SPLIT = 2, 4

ROW_CONV_W, ROW_MIX, ROW_X, ROW_MEM, ROW_FINAL = 0, 31, 33, 35, 37
ROW_CONV_B, ROW_LN_G, ROW_LN_B, ROW_POOL, ROW_SHORT = 38, 39, 40, 41, 42
ROWS = 48


class Core:
    pass


def place(c):
    nc = c.nc
    c.at = 16512
    c.X = persistent(c, "x_res", [P, KD, TP], F32)
    c.Hh = persistent(c, "h_hi", [P, KD, TP], F32R)
    c.Hl = persistent(c, "h_lo", [P, KD, TP], F32R)
    c.Yh = persistent(c, "y_hi", [P, 2, TP], F32R)
    c.Yl = persistent(c, "y_lo", [P, 2, TP], F32R)
    c.Wraw = persistent(c, "w_raw", [P, RAW, UNIT], F32)
    c.Wh = persistent(c, "w_hi", [P, SPLIT, UNIT], F32R)
    c.Wl = persistent(c, "w_lo", [P, SPLIT, UNIT], F32R)
    c.ident = persistent(c, "ident", [P, P], F32)
    c.ones = persistent(c, "ones", [P, P], F32)
    c.prm = persistent(c, "prm", [P, KD, ROWS], F32)
    c.eps = persistent(c, "eps", [P, 1], F32)
    c.region = c.at


def persistent(c, name, shape, dtype):
    size = 4
    for n in shape[1:]:
        size *= n
    t = c.nc.alloc_sbuf_tensor_at(name, shape, dtype, offset=c.at, align_bytes=16)
    c.at += (size + 15) // 16 * 16
    return t


def semaphores(c, ctx, prefix=""):
    given = []

    def sem(name):
        given.append(c.nc.alloc_semaphore(prefix + name))
        return given[-1]

    ctx.callback(c.nc.all_engine_barrier)
    ctx.callback(lambda: c.nc.clear_and_free_semaphores(given))
    return sem


def lay(c, name, shape, dtype=F32):
    return persistent(c, name, shape, dtype)


def group(c, b):
    return c.PS[:, 3 * b:3 * b + 3, :]


def parts(ap):
    return ap.rearrange("p (a n) -> p a n", a=3)


class Gemm:

    def __init__(self, c, sem):
        self.c = c
        self.raw_in = [sem(f"raw_in{i}") for i in range(RAW)]
        self.w_hi = sem("w_hi")
        self.w_split = sem("w_split")
        self.half = sem("half")
        self.freed = [sem(f"freed{i}") for i in range(2)]

    def load(self, sp, u, slot, src, wait=True):
        if wait:
            sp.wait_ge(self.w_split, u - RAW + 1)
        sp.dma_start(self.c.Wraw[:, slot % RAW, :].rearrange("p (a n) -> p a n", n=src.shape[-1]),
                     src).then_inc(self.raw_in[slot % RAW], 16)

    def split_one(self, pool, raw_count, u, s, used):
        c = self.c
        pool.wait_ge(self.raw_in[s % RAW], raw_count)
        if used is not None:
            pool.wait_ge(self.half, used)
        by_128 = lambda ap: ap.rearrange("p (a n) -> p a n", n=P)
        ones = c.ones[:, :].unsqueeze(1).to_broadcast([P, UNIT // P, P])
        c.nc.gpsimd.tensor_tensor(by_128(c.Wh[:, s, :]), by_128(c.Wraw[:, s % RAW, :]), ones,
                                  ALU.mult).then_inc(self.w_hi, 1)
        pool.wait_ge(self.w_hi, u + 1)
        c.nc.gpsimd.tensor_tensor(c.Wl[:, s, :], c.Wraw[:, s % RAW, :], c.Wh[:, s, :].bitcast(F32),
                                  ALU.subtract).then_inc(self.w_split, 1)

    def split_all(self, pool, units):
        for s in range(SPLIT):
            self.split_one(pool, 16 * (s // RAW + 1), s, s, None)
        with pool.Fori(1, units // SPLIT) as i:
            for s in range(SPLIT):
                self.split_one(pool, i * 32 + 16 * (s // RAW + 1), i * SPLIT + s, s, i * 8 + 2 * s - 6)

    def in_tile(self, pe, u, slot, b, freed, k_ready=None):
        c = self.c
        ps = group(c, b)
        if freed is not None:
            pe.wait_ge(self.freed[b], freed)
        for k in range(KD):
            s = (slot + k // 4) % SPLIT
            if k % 4 == 0:
                pe.wait_ge(self.w_split, u + k // 4 + 1)
            if k_ready is not None:
                pe.wait_ge(k_ready, k + 1)
            cols = slice(P * (k % 4), P * (k % 4 + 1))
            three_passes(pe, ps, c.Wh[:, s, cols], c.Wl[:, s, cols], c.Hh[:, k, :], c.Hl[:, k, :],
                         k == 0, k == KD - 1, self.half if k % 2 else None)

    def pair_tile(self, pe, slot, e, b, freed, Ah, Al):
        c = self.c
        if freed is not None:
            pe.wait_ge(self.freed[b], freed)
        s = slot % SPLIT
        for k in range(2):
            cols = slice(256 * k + P * e, 256 * k + P * (e + 1))
            three_passes(pe, group(c, b), c.Wh[:, s, cols], c.Wl[:, s, cols], Ah[:, k, :], Al[:, k, :],
                         k == 0, k == 1, self.half if k else None)


def three_passes(pe, ps, wh, wl, ah, al, first, last, signal):
    for w, a, n in ((wh, ah, 0), (wh, al, 1), (wl, ah, 2)):
        for q in range(3):
            mm = pe.matmul(ps[:, q, 0:PART], w, a[:, q * PART:(q + 1) * PART],
                           start=first and n == 0, stop=last and n == 2)
    if signal is not None:
        mm.then_inc(signal, 1)


def in_units(w, col):
    v = w.rearrange("(h k p) n -> h p k n", h=2, p=P)
    return [v[h, :, :, bass.ds(col, P)] for h in range(2)]


def out_units(w, row):
    return [w[bass.ds(row, 256), 256 * q:256 * (q + 1)].rearrange("(k p) n -> p k n", p=P) for q in range(4)]


class Norm:
    def __init__(self, c, sem, name):
        self.c = c
        self.sq, self.acc = sem("norm_sq"), sem("norm_acc")
        self.sum, self.std, self.rstd = sem("norm_sum"), sem("norm_std"), sem("norm_rstd")
        self.t, self.hi, self.lo = sem("norm_t"), sem("norm_hi"), sem("norm_lo")
        self.SQ = lay(c, f"{name}_SQ", [P, 2, TP])
        self.ACC = lay(c, f"{name}_ACC", [P, TP])
        self.R = lay(c, f"{name}_R", [P, TP])

    def scalar(self, act, split=True):
        c = self.c
        for k in range(KD):
            if k >= 2:
                act.wait_ge(self.acc, max(1, k - 2))
            c.nc.scalar.activation(self.SQ[:, k % 2, :], c.X[:, k, :], ACT.Square).then_inc(self.sq, 1)
        act.wait_ge(self.sum, 1)
        c.nc.scalar.activation(parts(self.R[:, :]), group(c, 1)[:, :, 0:PART], ACT.Sqrt,
                               bias=c.eps[:, 0:1], scale=1.0 / D).then_inc(self.std, 1)
        if split:
            for k in range(KD):
                act.wait_ge(self.t, k + 1)
                c.nc.scalar.activation(c.Hh[:, k, :], self.SQ[:, k % 2, :], ACT.Copy).then_inc(self.hi, 1)

    def tensor(self, pe):
        pe.wait_ge(self.acc, KD - 1)
        for q in range(3):
            mm = pe.matmul(group(self.c, 1)[:, q, 0:PART], self.c.ones[:, :],
                           self.ACC[:, q * PART:(q + 1) * PART], start=True, stop=True)
        mm.then_inc(self.sum, 1)

    def vector_rstd(self, dve):
        c = self.c
        dve.wait_ge(self.sq, 2)
        c.nc.vector.tensor_tensor(self.ACC[:, :], self.SQ[:, 0, :], self.SQ[:, 1, :], ALU.add).then_inc(self.acc, 1)
        for k in range(2, KD):
            dve.wait_ge(self.sq, k + 1)
            dve.wait_ge(self.acc, k - 1)
            c.nc.vector.tensor_tensor(self.ACC[:, :], self.ACC[:, :], self.SQ[:, k % 2, :],
                                      ALU.add).then_inc(self.acc, 1)
        dve.wait_ge(self.std, 1)
        c.nc.vector.reciprocal(self.R[:, :], self.R[:, :]).then_inc(self.rstd, 1)
        dve.wait_ge(self.rstd, 1)

    def vector(self, dve, row):
        c = self.c
        self.vector_rstd(dve)
        dve.wait_ge(self.acc, KD - 1)

        def low(k):
            dve.wait_ge(self.hi, k + 1)
            c.nc.vector.tensor_tensor(c.Hl[:, k, :], self.SQ[:, k % 2, :], c.Hh[:, k, :].bitcast(F32),
                                      ALU.subtract).then_inc(self.lo, 1)

        for k in range(KD):
            if k >= 2:
                dve.wait_ge(self.lo, k - 1)
            c.nc.vector.scalar_tensor_tensor(self.SQ[:, k % 2, :], c.X[:, k, :], c.prm[:, k, row:row + 1],
                                             self.R[:, :], ALU.mult, ALU.mult).then_inc(self.t, 1)
            if k >= 1:
                low(k - 1)
        low(KD - 1)


def block_load(c):
    nc = c.nc
    c.at = c.region
    PR = lay(c, "prm_rows", [P, D])
    XN = lay(c, "x_rows", [P, 2, D])
    with ExitStack() as ctx:
        sem = semaphores(c, ctx)
        prm_in, ident_zero, ident_made, const_made = sem("prm_in"), sem("ident_zero"), sem("ident_made"), sem("const_made")
        x_in = [sem(f"x_in{i}") for i in range(2)]
        turned = sem("x_turned")
        copied = [sem("x_copied0"), sem("x_copied1")]
        rows_copied = sem("prm_copied")
        block = ctx.enter_context(nc.Block())
        tiles = T // P + 1

        @block.sync
        def _(sp):
            r = c.dram
            for row, n, ap in ((ROW_CONV_W, CONV, r["conv_w"][0]), (ROW_MIX, 2, r["norm_mix"]), (ROW_X, 2, r["norm_x"]),
                               (ROW_MEM, 2, r["norm_mem"]), (ROW_FINAL, 1, r["final_norm"].rearrange("(a d) -> a d", a=1)),
                               (ROW_CONV_B, 1, r["conv_b"]), (ROW_LN_G, 1, r["ln_g"]), (ROW_LN_B, 1, r["ln_b"]),
                               (ROW_POOL, 1, r["pool_scale"]),
                               (ROW_SHORT, 6, r["short_w"][0].rearrange("t (h d) -> (t h) d", h=2))):
                sp.dma_start(PR[row:row + n, :], ap).then_inc(prm_in, 16)
            for t in range(tiles):
                if t >= 2:
                    sp.wait_ge(turned, 2 + 2 * (t - 1))
                if t < T // P:
                    sp.dma_start(XN[:, t % 2, :], r["x_prompt"][0, t * P:(t + 1) * P, :]).then_inc(x_in[t % 2], 16)
                else:
                    sp.dma_start(XN[0:NS, t % 2, :], r["x_sample"].rearrange("b t d -> (b t) d")).then_inc(x_in[t % 2], 16)

        @block.gpsimd
        def _(pool):
            nc.gpsimd.memset(c.ident[:, :], 0.0).then_inc(ident_zero, 1)
            pool.wait_ge(ident_zero, 1)
            nc.gpsimd.affine_select(out=c.ident[:, :], in_=c.ident[:, :], compare_op=ALU.not_equal, fill=1.0,
                                    base=0, pattern=[[-1, P]], channel_multiplier=1).then_inc(ident_made, 1)

        @block.tensor
        def _(pe):
            pe.wait_ge(ident_made, 1)
            pe.wait_ge(prm_in, 160)
            for h in range(2):
                for k in range(4):
                    mm = pe.transpose(c.PS[:, h, k * ROWS:(k + 1) * ROWS], PR[0:ROWS, (4 * h + k) * P:(4 * h + k + 1) * P],
                                      c.ident[0:ROWS, 0:ROWS])
                mm.then_inc(turned, 1)
            for t in range(tiles):
                n = P if t < T // P else NS
                pe.wait_ge(x_in[t % 2], 16 * (t // 2 + 1))
                for h in range(2):
                    if t >= 2:
                        pe.wait_ge(copied[h], t - 1)
                    for k in range(4):
                        mm = pe.transpose(c.PS[:, 2 + 2 * (t % 2) + h, k * P:k * P + n],
                                          XN[0:n, t % 2, (4 * h + k) * P:(4 * h + k + 1) * P], c.ident[0:n, 0:n])
                    mm.then_inc(turned, 1)

        @block.scalar
        def _(act):
            for t in range(tiles):
                n = P if t < T // P else NS
                act.wait_ge(turned, 2 + 2 * t + 1)
                src = c.PS[:, 2 + 2 * (t % 2), :].rearrange("p (k n) -> p k n", k=4)[:, :, 0:n]
                nc.scalar.activation(c.X[:, 0:4, t * P:t * P + n], src, ACT.Copy).then_inc(copied[0], 1)

        @block.vector
        def _(dve):
            nc.vector.memset(c.ones[:, :], 1.0).then_inc(const_made, 1)
            nc.vector.memset(c.eps[:, :], EPS).then_inc(const_made, 1)
            nc.vector.memset(c.X[:, :, TA:TP], 0.0).then_inc(const_made, 1)
            for h in range(2):
                dve.wait_ge(turned, h + 1)
                nc.vector.tensor_copy(c.prm[:, 4 * h:4 * h + 4, :],
                                      c.PS[:, h, 0:4 * ROWS].rearrange("p (k n) -> p k n", k=4)).then_inc(rows_copied, 1)
            for t in range(tiles):
                n = P if t < T // P else NS
                dve.wait_ge(turned, 2 + 2 * t + 2)
                src = c.PS[:, 3 + 2 * (t % 2), :].rearrange("p (k n) -> p k n", k=4)[:, :, 0:n]
                nc.vector.tensor_copy(c.X[:, 4:8, t * P:t * P + n], src).then_inc(copied[1], 1)


def block_final(c):
    nc = c.nc
    c.at = c.region
    XF = lay(c, "x_final", [P, KD, TP])
    YN = lay(c, "y_rows", [P, 2, D])
    tiles = T // P + 1
    with ExitStack() as ctx:
        sem = semaphores(c, ctx)
        norm = Norm(c, sem, "nf")
        scaled, turned, stored = sem("scaled"), sem("y_turned"), [sem("y_stored0"), sem("y_stored1")]
        copied = [sem("y_copied0"), sem("y_copied1")]
        block = ctx.enter_context(nc.Block())

        @block.scalar
        def _(act):
            norm.scalar(act, split=False)
            for t in range(tiles):
                n = P if t < T // P else NS
                act.wait_ge(turned, 2 * t + 1)
                if t >= 2:
                    act.wait_ge(stored[t % 2], 16 * (t // 2))
                nc.scalar.activation(YN[0:n, t % 2, 0:512], c.PS[0:n, 2 * (t % 2), :], ACT.Copy).then_inc(copied[0], 1)

        @block.tensor
        def _(pe):
            norm.tensor(pe)
            pe.wait_ge(scaled, KD)
            for t in range(tiles):
                n = P if t < T // P else NS
                for h in range(2):
                    if t >= 2:
                        pe.wait_ge(copied[h], t - 1)
                    for k in range(4):
                        mm = pe.transpose(c.PS[0:n, 2 * (t % 2) + h, k * P:(k + 1) * P],
                                          XF[:, 4 * h + k, t * P:t * P + n], c.ident[:, :])
                    mm.then_inc(turned, 1)

        @block.vector
        def _(dve):
            norm.vector_rstd(dve)
            for k in range(KD):
                nc.vector.scalar_tensor_tensor(XF[:, k, :], c.X[:, k, :], c.prm[:, k, ROW_FINAL:ROW_FINAL + 1],
                                               norm.R[:, :], ALU.mult, ALU.mult).then_inc(scaled, 1)
            for t in range(tiles):
                n = P if t < T // P else NS
                dve.wait_ge(turned, 2 * t + 2)
                if t >= 2:
                    dve.wait_ge(stored[t % 2], 16 * (t // 2))
                nc.vector.tensor_copy(YN[0:n, t % 2, 512:1024], c.PS[0:n, 2 * (t % 2) + 1, :]).then_inc(copied[1], 1)

        @block.sync
        def _(sp):
            for t in range(tiles):
                sp.wait_ge(copied[0], t + 1)
                sp.wait_ge(copied[1], t + 1)
                if t < T // P:
                    sp.dma_start(c.dram["y_prompt"][0, t * P:(t + 1) * P, :], YN[:, t % 2, :]).then_inc(stored[t % 2], 16)
                else:
                    sp.dma_start(c.dram["y_sample"].rearrange("b t d -> (b t) d"), YN[0:NS, t % 2, :]).then_inc(stored[t % 2], 16)
            sp.wait_ge(stored[0], 16 * ((tiles + 1) // 2))
            sp.wait_ge(stored[1], 16 * (tiles // 2))
def even_plan():
    order = []
    for g in range(4):
        order += [(n, 2 * g) for n in ("glu", "val", "ain", "agate")]
        if g:
            order += [("outa", g - 1, k) for k in range(KD)]
        order += [(n, 2 * g + 1) for n in ("glu", "val", "ain", "agate")]
        order += [("pool", 2 * g), ("pool", 2 * g + 1)]
    order += [("bgate", 0), ("bgate", 1)]
    order += [("outa", 3, k) for k in range(KD)]
    order += [("sum", 0), ("sum", 1)]
    for g in range(4):
        if g < 3:
            order += [("bgate", 2 * g + 2), ("bgate", 2 * g + 3)]
        order += [("outb", g, k) for k in range(KD)]
    number, end, half = {}, {}, 0
    for n, tile in enumerate(order):
        half += {"outa": 1, "outb": 1, "pool": 1, "sum": 0}.get(tile[0], 4)
        number[tile], end[tile] = n, half
    return order, number, end


def block_even(c):
    nc, r = c.nc, c.dram
    c.at = c.region
    order, number, end = even_plan()
    w_in, w_out = r["w_in_even"][0], r["w_out_even"][0]
    conv_rows = r["state_conv"][0].rearrange("b t c -> (b t) c")
    pool_rows = r["state_pool"][0].rearrange("b t c -> (b t) c")
    new_conv = r["new_conv_sample"][0].rearrange("b t c -> (b t) c")
    new_pool = r["new_pool_sample"][0].rearrange("b t c -> (b t) c")
    CR, PR = NB * HC // 2, NB * HPOOL
    scratch = r["conv_scratch"]
    TAPS = 2 * CONV
    with ExitStack() as ctx:
        sem = semaphores(c, ctx, f"e_")
        norm = Norm(c, sem, "en")
        c.at = c.region
        V = lay(c, "e_V", [P, HC + TP])
        SG = lay(c, "e_SG", [P, TP])
        GS = lay(c, "e_GS", [P, 2, TP])
        A = lay(c, "e_A", [P, HPOOL + TP])
        PT = lay(c, "e_P", [P, TP])
        CB = lay(c, "e_C", [P, 2, TP])
        S1 = lay(c, "e_S1", [P, TP])
        S2 = lay(c, "e_S2", [P, TP])
        Mh = lay(c, "e_Mh", [P, 2, TP], F32R)
        Ml = lay(c, "e_Ml", [P, 2, TP], F32R)
        VS = lay(c, "e_VS", [P, NB, HC + TS])
        AS = lay(c, "e_AS", [P, NB, HPOOL + TS])
        HN = lay(c, "e_HN", [P, 3, P])
        OS = lay(c, "e_OS", [P, 5, P])
        AT = SG[:, 0:184].rearrange("p (b t) -> p b t", b=NB)
        TC = SG[:, 184:424]
        TA_ = SG[:, 424:544]
        G = Gemm(c, sem)
        hist_in, hist_turned, hist_copied = sem("hist_in"), sem("hist_turned"), sem("hist_copied")
        vs_new, as_new, tail_side = sem("vs_new"), sem("as_new"), sem("tail_side")
        tails_turned, rows_copied, rows_stored = sem("tails_turned"), sem("rows_copied"), sem("rows_stored")
        cv, stats, stored = sem("cv"), sem("stats"), [sem("c_stored0"), sem("c_stored1")]
        level, m_done, m_hi, m_lo, y_hi, y_lo = sem("level"), sem("m_done"), sem("m_hi"), sem("m_lo"), sem("y_hi"), sem("y_lo")
        init, ln_sum, ln_sq, ln_var, ln_std, ln_r = sem("init"), sem("ln_sum"), sem("ln_sq"), sem("ln_var"), sem("ln_std"), sem("ln_r")
        c_in, centred, ln_x, ln_y, yb = [sem("c_in0"), sem("c_in1")], sem("centred"), sem("ln_x"), sem("ln_y"), sem("yb")
        block = ctx.enter_context(nc.Block())

        def bank(tile):
            return group(c, number[tile] % 2)[:, :, 0:PART]

        def wait_result(e, tile):
            e.wait_ge(G.half, end[tile])

        def freed(tile):
            return G.freed[number[tile] % 2]

        def wait_read(e, tile):
            e.wait_ge(freed(tile), number[tile] // 2 + 1)

        @block.sync
        def _(sp):
            u = 0
            for tile in order:
                kind, j = tile[0], tile[1]
                if kind == "glu":
                    if j:
                        sp.wait_ge(hist_turned, j)
                    cols = slice(j * P, (j + 1) * P)
                    sp.dma_start(HN[0:CR, 0:2, :], conv_rows[:, cols].rearrange("(h p) c -> p h c", h=2)).then_inc(hist_in, 16)
                    sp.dma_start(HN[0:PR, 2, :], pool_rows[:, cols]).then_inc(hist_in, 16)
                if kind in ("glu", "val", "ain", "agate", "bgate"):
                    part = {"ain": 0, "agate": 1, "val": 2, "glu": 3, "bgate": 4}[kind]
                    for src in in_units(w_in, part * WB + j * P):
                        G.load(sp, u, u, src, wait=u >= RAW)
                        u += 1
                elif kind == "pool" and j % 2 == 0:
                    G.load(sp, u, u, r["pool_w"][0, j // 2].rearrange("(k p) n -> p k n", p=P))
                    u += 1
                elif kind in ("outa", "outb") and tile[2] == 0:
                    for src in out_units(w_out, (WB if kind == "outb" else 0) + 256 * j):
                        G.load(sp, u, u, src)
                        u += 1
                if kind == "sum" and j == 1 or kind == "outb" and tile[2] == 0 and j < 3:
                    for n in (0, 1) if kind == "sum" else (2 * j + 2, 2 * j + 3):
                        if n < 2:
                            sp.wait_ge(stored[n], 16 * KD // 2)
                            sp.wait_ge(stats, 3 * (7 + n))
                        else:
                            sp.wait_ge(yb, n - 1)
                        sp.dma_start(CB[:, n % 2, :], scratch[n]).then_inc(c_in[n % 2], 16)
            sp.wait_ge(rows_stored, 80 * KD)

        @block.gpsimd
        def _(pool):
            G.split_all(pool, 116)

        @block.tensor
        def _(pe):
            def tails(j):
                pe.wait_ge(tail_side, 2 * (j + 1))
                pe.wait_ge(hist_copied, 2 * (j + 1))
                if j:
                    pe.wait_ge(rows_copied, 5 * j)
                out = c.PS[:, 7, :].rearrange("p (n m) -> p n m", n=4)
                pe.transpose(out[0:HC, 0, :], V[:, T:T + HC], c.ident[:, :])
                pe.transpose(out[0:CR, 1, :], TC[:, 0:CR], c.ident[:, :])
                pe.transpose(out[0:CR, 2, :], TC[:, CR:2 * CR], c.ident[:, :])
                pe.transpose(out[0:HPOOL, 3, :], A[:, T:T + HPOOL], c.ident[:, :])
                pe.transpose(c.PS[0:PR, 6, 384:512], TA_, c.ident[:, :]).then_inc(tails_turned, 1)

            def history(j):
                pe.wait_ge(hist_in, 32 * (j + 1))
                if j:
                    pe.wait_ge(hist_copied, 2 * j)
                if j >= 2:
                    pe.wait_ge(rows_copied, 5 * (j - 1))
                for h in range(3):
                    mm = pe.transpose(c.PS[:, 6, h * CR:(h + 1) * CR], HN[0:CR, h, :], c.ident[0:CR, 0:CR])
                mm.then_inc(hist_turned, 1)

            norm.tensor(pe)
            u = 0
            for tile in order:
                kind, j, n = tile[0], tile[1], number[tile]
                before = n // 2 if n >= 2 else None
                if kind in ("glu", "val", "ain", "agate", "bgate"):
                    G.in_tile(pe, u, u, n % 2, before, norm.lo if n == 0 else None)
                    u += 2
                    if kind == "glu":
                        history(j)
                        if j:
                            tails(j - 1)
                    if tile == ("bgate", 0):
                        tails(KD - 1)
                elif kind == "sum":
                    pe.wait_ge(stats, 3 * KD)
                    pe.wait_ge(freed(tile), before)
                    for q in range(3):
                        mm = pe.matmul(group(c, n % 2)[:, q, 0:PART], c.ones[:, :],
                                       (S1, S2)[j][:, q * PART:(q + 1) * PART], start=True, stop=True)
                    mm.then_inc(ln_sum, 1)
                else:
                    k = j % 2 if kind == "pool" else tile[2]
                    if kind == "pool":
                        pe.wait_ge(m_lo, j + 1 + (1 - k))
                    else:
                        pe.wait_ge(y_lo, 2 * j + 2 + (KD if kind == "outb" else 0))
                    if k % 2 == 0:
                        pe.wait_ge(G.w_split, u + 1)
                    Ah, Al = (Mh, Ml) if kind == "pool" else (c.Yh, c.Yl)
                    G.pair_tile(pe, u, k % 2, n % 2, before, Ah, Al)
                    u += k % 2

        @block.scalar
        def _(act):
            s = nc.scalar

            def evacuate(tile, out, func, **more):
                wait_result(act, tile)
                s.activation(parts(out), bank(tile), func, **more).then_inc(freed(tile), 1)

            def store_conv(j):
                act.wait_ge(cv, TAPS * (j + 1))
                act.dma_start(scratch[j], CB[:, j % 2, :]).then_inc(stored[j % 2], 16)

            def history(j):
                act.wait_ge(hist_turned, j + 1)
                s.activation(VS[:, :, 0:HC], c.PS[:, 6, 0:NB * HC].rearrange("p (b t) -> p b t", b=NB),
                             ACT.Copy).then_inc(hist_copied, 1)
                s.activation(AS[:, :, 0:HPOOL], c.PS[:, 6, 2 * CR:2 * CR + PR].rearrange("p (b t) -> p b t", b=NB),
                             ACT.Copy).then_inc(hist_copied, 1)

            def conv_tail(j):
                act.wait_ge(vs_new, j + 1)
                act.wait_ge(hist_copied, 2 * j + 2)
                s.activation(TC.rearrange("p (b t) -> p b t", b=NB), VS[:, :, TS:HC + TS], ACT.Copy).then_inc(tail_side, 1)

            def pool_tail(j):
                act.wait_ge(as_new, j + 1)
                s.activation(TA_.rearrange("p (b t) -> p b t", b=NB), AS[:, :, TS:HPOOL + TS], ACT.Copy).then_inc(tail_side, 1)

            def store_tails(j):
                act.wait_ge(tails_turned, j + 1)
                if j:
                    act.wait_ge(rows_stored, 80 * j)
                for n, rows in enumerate((HC, CR, CR, HPOOL)):
                    s.activation(OS[0:rows, n, :], c.PS[0:rows, 7, n * P:(n + 1) * P], ACT.Copy).then_inc(rows_copied, 1)
                s.activation(OS[0:PR, 4, :], c.PS[0:PR, 6, 384:512], ACT.Copy).then_inc(rows_copied, 1)
                act.wait_ge(rows_copied, 5 * (j + 1))
                cols = slice(j * P, (j + 1) * P)
                act.dma_start(r["new_conv_prompt"][0, 0, :, cols], OS[0:HC, 0, :]).then_inc(rows_stored, 16)
                act.dma_start(new_conv[0:CR, cols], OS[0:CR, 1, :]).then_inc(rows_stored, 16)
                act.dma_start(new_conv[CR:2 * CR, cols], OS[0:CR, 2, :]).then_inc(rows_stored, 16)
                act.dma_start(r["new_pool_prompt"][0, 0, :, cols], OS[0:HPOOL, 3, :]).then_inc(rows_stored, 16)
                act.dma_start(new_pool[:, cols], OS[0:PR, 4, :]).then_inc(rows_stored, 16)

            def pooled_high(j):
                act.wait_ge(m_done, j + 1)
                if j >= 2:
                    wait_result(act, ("pool", 2 * (j // 2) - 1))
                s.activation(Mh[:, j % 2, :], PT[:, :], ACT.Copy).then_inc(m_hi, 1)

            def ya_high(j):
                wait_read(act, ("pool", j))
                if j >= 2:
                    wait_result(act, ("outa", j // 2 - 1, KD - 1))
                s.activation(c.Yh[:, j % 2, :], PT[:, :], ACT.Copy).then_inc(y_hi, 1)

            norm.scalar(act)
            for j in range(KD):
                if j:
                    store_tails(j - 1)
                if j % 2 == 0 and j:
                    ya_high(j - 2)
                    ya_high(j - 1)
                evacuate(("glu", j), SG[:, :], ACT.Sigmoid)
                if j:
                    store_conv(j - 1)
                history(j)
                conv_tail(j)
                if j:
                    act.wait_ge(m_lo, j)
                evacuate(("ain", j), A[:, HPOOL:HPOOL + TP], ACT.Copy)
                if j >= 2:
                    wait_read(act, ("pool", j - 2))
                evacuate(("agate", j), GS[:, j % 2, :], ACT.Silu)
                pool_tail(j)
                pooled_high(j)
            ya_high(KD - 2)
            ya_high(KD - 1)

            def yb_high(j):
                act.wait_ge(yb, j + 1)
                wait_result(act, ("outb", j // 2 - 1, KD - 1) if j >= 2 else ("outa", 3, KD - 1))
                s.activation(c.Yh[:, j % 2, :], PT[:, :], ACT.Copy).then_inc(y_hi, 1)

            def swish(j):
                act.wait_ge(ln_x, j + 1)
                s.activation(CB[:, j % 2, :], CB[:, j % 2, :], ACT.Silu, bias=c.prm[:, j, ROW_LN_B:ROW_LN_B + 1],
                             scale=c.prm[:, j, ROW_LN_G:ROW_LN_G + 1]).then_inc(ln_y, 1)

            for j in range(2):
                wait_read(act, ("pool", KD - 2 + j))
                evacuate(("bgate", j), GS[:, j, :], ACT.Silu)
                if j == 0:
                    store_tails(KD - 1)
            store_conv(KD - 1)
            act.wait_ge(ln_sum, 1)
            s.activation(parts(SG[:, :]), bank(("sum", 0)), ACT.Copy, scale=1.0 / WB).then_inc(freed(("sum", 0)), 1)
            act.wait_ge(ln_var, 1)
            s.activation(V[:, 0:TP], V[:, 0:TP], ACT.Sqrt, bias=c.eps[:, 0:1]).then_inc(ln_std, 1)
            swish(0)
            swish(1)
            for g in range(4):
                yb_high(2 * g)
                yb_high(2 * g + 1)
                if g < 3:
                    for j in (2 * g + 2, 2 * g + 3):
                        evacuate(("bgate", j), GS[:, j % 2, :], ACT.Silu)
                    swish(2 * g + 2)
                    swish(2 * g + 3)

        @block.vector
        def _(dve):
            v = nc.vector
            sums = [0]

            def next_level(instruction, of=None):
                instruction.then_inc(level, 1)
                sums[0] += 1
                dve.wait_ge(level, sums[0])

            def value(j):
                wait_result(dve, ("val", j))
                wait_read(dve, ("glu", j))
                if j:
                    dve.wait_ge(tails_turned, j)
                    dve.wait_ge(cv, TAPS * j)
                v.tensor_tensor(parts(V[:, HC:HC + TP]), bank(("val", j)), parts(SG[:, :]),
                                ALU.mult).then_inc(freed(("val", j)), 1)
                wait_read(dve, ("val", j))
                v.tensor_copy(VS[:, :, HC:HC + TS], V[:, HC + T:HC + TA].rearrange("p (b t) -> p b t", b=NB)).then_inc(vs_new, 1)

            def conv(j, first, last):
                if first == 0:
                    dve.wait_ge(hist_copied, 2 * j + 2)
                    dve.wait_ge(vs_new, j + 1)
                    if j >= 2:
                        dve.wait_ge(stored[j % 2], 16 * (j // 2))
                        dve.wait_ge(stats, 3 * (j - 1))
                outs = (CB[:, j % 2, 0:T], CB[:, j % 2, T:TA].rearrange("p (b t) -> p b t", b=NB))
                for n in range(first, last):
                    ins = (V[:, n:n + T], VS[:, :, n:n + TS])
                    tap = c.prm[:, j, ROW_CONV_W + n:ROW_CONV_W + n + 1]
                    for i in range(2):
                        if n == 0:
                            v.tensor_scalar(outs[i], ins[i], tap, c.prm[:, j, ROW_CONV_B:ROW_CONV_B + 1],
                                            ALU.mult, ALU.add).then_inc(cv, 1)
                        else:
                            dve.wait_ge(cv, TAPS * j + 2 * (n - 1) + i + 1)
                            v.scalar_tensor_tensor(outs[i], ins[i], tap, outs[i], ALU.mult, ALU.add).then_inc(cv, 1)

            def add_stats(j):
                dve.wait_ge(cv, TAPS * (j + 1))
                C = CB[:, j % 2, :]
                if j == 0:
                    v.tensor_copy(S1[:, :], C).then_inc(stats, 1)
                    v.tensor_tensor(S2[:, :], C, C, ALU.mult).then_inc(stats, 1)
                    v.tensor_copy(PT[:, 0:1], PT[:, TA:TA + 1]).then_inc(stats, 1)
                else:
                    dve.wait_ge(stats, 3 * j)
                    v.tensor_tensor(S1[:, :], S1[:, :], C, ALU.add).then_inc(stats, 1)
                    v.tensor_tensor(PT[:, :], C, C, ALU.mult).then_inc(stats, 1)
                    dve.wait_ge(stats, 3 * j + 2)
                    v.tensor_tensor(S2[:, :], S2[:, :], PT[:, :], ALU.add).then_inc(stats, 1)

            def pooling(j):
                w = 2 << j // 2
                wait_read(dve, ("ain", j))
                dve.wait_ge(hist_copied, 2 * j + 2)
                v.tensor_copy(AS[:, :, HPOOL:HPOOL + TS], A[:, HPOOL + T:HPOOL + TA].rearrange("p (b t) -> p b t", b=NB)
                              ).then_inc(as_new, 1)
                n = HPOOL + T
                next_level(v.tensor_tensor(PT[:, 0:n - 1], A[:, 0:n - 1], A[:, 1:n], ALU.add))
                dve.wait_ge(as_new, j + 1)
                dve.wait_ge(vs_new, j + 1)
                m = HPOOL + TS
                next_level(v.tensor_tensor(AT[:, :, 0:m - 1], AS[:, :, 0:m - 1], AS[:, :, 1:m], ALU.add))
                n, m, s = n - 1, m - 1, 2
                while s < w:
                    next_level(v.tensor_tensor(PT[:, 0:n - s], PT[:, 0:n - s], PT[:, s:n], ALU.add))
                    next_level(v.tensor_tensor(AT[:, :, 0:m - s], AT[:, :, 0:m - s], AT[:, :, s:m], ALU.add))
                    n, m, s = n - s, m - s, 2 * s
                for t in range(w - 1):
                    i = 16 - w + t
                    v.scalar_tensor_tensor(PT[:, t:t + 1], PT[:, i:i + 1], 1.0 / (t + 1), A[:, HPOOL + t:HPOOL + t + 1],
                                           ALU.mult, ALU.subtract).then_inc(level, 1)
                    sums[0] += 1
                dve.wait_ge(level, sums[0])
                next_level(v.scalar_tensor_tensor(PT[:, w - 1:T], PT[:, 15:16 - w + T], 1.0 / w, A[:, HPOOL + w - 1:HPOOL + T],
                                                  ALU.mult, ALU.subtract))
                v.scalar_tensor_tensor(PT[:, T:TA].rearrange("p (b t) -> p b t", b=NB), AT[:, :, 16 - w:16 - w + TS], 1.0 / w,
                                       AS[:, :, HPOOL:HPOOL + TS], ALU.mult, ALU.subtract).then_inc(m_done, 1)

            def pooled_low(j):
                dve.wait_ge(m_hi, j + 1)
                v.tensor_tensor(Ml[:, j % 2, :], PT[:, :], Mh[:, j % 2, :].bitcast(F32), ALU.subtract).then_inc(m_lo, 1)

            def ya(j):
                wait_result(dve, ("pool", j))
                wait_read(dve, ("agate", j))
                dve.wait_ge(m_lo, 2 * (j // 2) + 2)
                if j % 2:
                    dve.wait_ge(y_lo, j)
                v.scalar_tensor_tensor(parts(PT[:, :]), bank(("pool", j)), c.prm[:, j, ROW_POOL:ROW_POOL + 1],
                                       parts(GS[:, j % 2, :]), ALU.mult, ALU.mult).then_inc(freed(("pool", j)), 1)

            def y_low(j, n):
                dve.wait_ge(y_hi, n + 1)
                v.tensor_tensor(c.Yl[:, j % 2, :], PT[:, :], c.Yh[:, j % 2, :].bitcast(F32), ALU.subtract).then_inc(y_lo, 1)

            def add(kind, g, k):
                tile = (kind, g, k)
                wait_result(dve, tile)
                v.tensor_tensor(parts(c.X[:, k, :]), bank(tile), parts(c.X[:, k, :]), ALU.add).then_inc(freed(tile), 1)

            norm.vector(dve, ROW_MIX)
            dve.wait_ge(norm.lo, KD)
            v.memset(V[:, 0:HC], 0.0).then_inc(init, 1)
            v.memset(A[:, 0:HPOOL], 0.0).then_inc(init, 1)
            v.memset(CB[:, :, TA:TP], 0.0).then_inc(init, 1)
            v.memset(PT[:, TA:TP], 0.0).then_inc(init, 1)
            dve.wait_ge(init, 4)
            for g in range(4):
                for e in range(2):
                    j = 2 * g + e
                    value(j)
                    if e == 0 and g:
                        conv(j, 0, 4)
                        at = 4
                    else:
                        conv(j, 0, 8)
                        at = 8
                    pooling(j)
                    conv(j, at, at + 2)
                    at += 2
                    pooled_low(j)
                    dve.wait_ge(m_lo, j + 1)
                    if e == 0 and g:
                        for k in range(KD):
                            add("outa", g - 1, k)
                            conv(j, at, at + 2)
                            at += 2
                    if e == 1:
                        conv(j, at, 20)
                        ya(j - 1)
                        conv(j, 20, 22)
                        y_low(j - 1, j - 1)
                        dve.wait_ge(y_lo, j)
                        ya(j)
                        conv(j, 22, 24)
                        y_low(j, j)
                        dve.wait_ge(y_lo, j + 1)
                        at = 24
                    conv(j, at, CONV)
                    add_stats(j)
            for k in range(KD):
                add("outa", 3, k)
            wait_read(dve, ("sum", 0))
            dve.wait_ge(stats, 3 * KD)
            v.tensor_tensor(PT[:, :], SG[:, :], SG[:, :], ALU.mult).then_inc(ln_sq, 1)
            dve.wait_ge(ln_sq, 1)
            dve.wait_ge(ln_sum, 2)
            dve.wait_ge(tails_turned, KD)
            dve.wait_ge(cv, TAPS * KD)
            v.scalar_tensor_tensor(parts(V[:, 0:TP]), bank(("sum", 1)), 1.0 / WB, parts(PT[:, :]), ALU.mult,
                                   ALU.subtract).then_inc(freed(("sum", 1)), 1)
            wait_read(dve, ("sum", 1))
            v.tensor_scalar(V[:, 0:TP], V[:, 0:TP], 0.0, None, ALU.max).then_inc(ln_var, 1)
            dve.wait_ge(ln_std, 1)
            v.reciprocal(V[:, 0:TP], V[:, 0:TP]).then_inc(ln_r, 1)
            dve.wait_ge(ln_r, 1)

            def normalise(j):
                dve.wait_ge(c_in[j % 2], 16 * (j // 2 + 1))
                v.tensor_tensor(CB[:, j % 2, :], CB[:, j % 2, :], SG[:, :], ALU.subtract).then_inc(centred, 1)
                dve.wait_ge(centred, j + 1)
                v.tensor_tensor(CB[:, j % 2, :], CB[:, j % 2, :], V[:, 0:TP], ALU.mult).then_inc(ln_x, 1)

            normalise(0)
            normalise(1)
            for g in range(4):
                for j in (2 * g, 2 * g + 1):
                    dve.wait_ge(ln_y, j + 1)
                    wait_read(dve, ("bgate", j))
                    if j:
                        dve.wait_ge(y_lo, KD + j)
                    v.tensor_tensor(PT[:, :], CB[:, j % 2, :], GS[:, j % 2, :], ALU.mult).then_inc(yb, 1)
                    y_low(j, KD + j)
                if g < 3:
                    normalise(2 * g + 2)
                    normalise(2 * g + 3)
                for k in range(KD):
                    if g == 0 and k == 0:
                        wait_read(dve, ("outa", 3, KD - 1))
                    add("outb", g, k)


def block_cross(c, layer):
    nc, r = c.nc, c.dram
    c.at = c.region
    name = f"a{layer}"
    TILES, HALVES, UNITS = 12, 32, 16
    NT = T // P
    w = {n: r[f"w_{n}"][layer] for n in "qkvo"}
    memory = r["mem_prompt"][0].rearrange("(a p) d -> p a d", p=P)
    with ExitStack() as ctx:
        sem = semaphores(c, ctx, f"{name}_")
        norm = Norm(c, sem, f"{name}n")
        after_norm = c.at
        c.at = c.region
        Q = lay(c, f"{name}_Q", [P, 2, TP])
        PT = lay(c, f"{name}_PT", [P, 2, T])
        E = lay(c, f"{name}_E", [P, 2, MEM])
        c.at = max(c.at, after_norm)
        KTS = lay(c, f"{name}_KTS", [P, 2, 2 * MEM])
        QM = lay(c, f"{name}_QM", [P, 2, NB * 72])
        end_of_rows = c.at
        c.at -= 4096 + 2 * NB * 72 * 4
        MN = lay(c, f"{name}_MN", [P, 2, D])
        c.at = end_of_rows
        MTh = lay(c, f"{name}_MTh", [P, KD, MEM], F32R)
        MTl = lay(c, f"{name}_MTl", [P, KD, MEM], F32R)
        KN = lay(c, f"{name}_KN", [P, 2, HD])
        VN = lay(c, f"{name}_VN", [P, 2, HD])
        KT = lay(c, f"{name}_KT", [P, 2, MEM])
        KV = lay(c, f"{name}_KV", [P, 4, 2 * HD])
        PTS = lay(c, f"{name}_PTS", [P, 2, NS + 4])
        ES = lay(c, f"{name}_ES", [NS, MEM])
        st = lay(c, f"{name}_st", [P, 16])
        NM, SUM, MS = st[:, 0:2], st[:, 2:4], st[:, 4:6]
        NMS, SUMS = st[0:NS, 6:7], st[0:NS, 7:8]
        G = Gemm(c, sem)
        mem_in, mem_sq, mem_std, mem_r, mem_n = sem("mem_in"), sem("mem_sq"), sem("mem_std"), sem("mem_r"), sem("mem_n")
        mem_turned, mt_hi, mt_lo, init = sem("mem_turned"), sem("mt_hi"), sem("mt_lo"), sem("init")
        kv_in = [sem(f"kv_in{i}") for i in range(4)]
        kt_turned, kt_copied, k_stored, v_stored, qm_set = sem("kt_turned"), sem("kt_copied"), sem("k_stored"), sem("v_stored"), sem("qm_set")
        scored, maxed, exped, inverted, weighed = sem("scored"), sem("maxed"), sem("exped"), sem("inverted"), sem("weighed")
        p_turned, p_copied = sem("p_turned"), sem("p_copied")
        ks_turned, ks_copied, s_scored = sem("ks_turned"), sem("ks_copied"), sem("s_scored")
        s_maxed, s_exped, s_inverted, s_weighed = sem("s_maxed"), sem("s_exped"), sem("s_inverted"), sem("s_weighed")
        s_turned, s_copied, v_used = sem("s_turned"), sem("s_copied"), sem("v_used")
        y_hi, y_lo = sem("y_hi"), sem("y_lo")
        block = ctx.enter_context(nc.Block())

        END = {0: 8, 1: 16, 2: 20, 3: 24, **{4 + k: 25 + k for k in range(KD)}}

        def wait_result(e, h, n):
            e.wait_ge(G.half, h * HALVES + END[n])

        def wait_read(e, h, n):
            e.wait_ge(G.freed[n % 2], h * (TILES // 2) + n // 2 + 1)

        def heads(e, body):
            body(0, True)
            with e.Fori(1, NH) as h:
                body(h, False)

        @block.sync
        def _(sp):
            sp.dma_start(MN[:, :, :], memory).then_inc(mem_in, 16)

            def head(h, first):
                def rows_256(m, u):
                    v = w[m].rearrange("(q k p) n -> q p k n", k=2, p=P)
                    for q in range(4):
                        G.load(sp, h * UNITS + u + q, q, v[q, :, :, bass.ds(h * HD, HD)], wait=not first or u + q >= RAW)

                rows_256("k", 0)
                rows_256("v", 4)
                for t in range(2):
                    for n, src in enumerate(in_units(w["q"], h * HD + t * P)):
                        G.load(sp, h * UNITS + 8 + 2 * t + n, n, src)

                def cached(b, which):
                    i = b + (NB if which == "v" else 0)
                    if b >= 4:
                        sp.wait_ge(ks_turned if which == "k" else v_used, h * NB + b - 3)
                    elif which == "v":
                        sp.wait_ge(ks_turned, h * NB + b + 5)
                    elif not first:
                        sp.wait_ge(v_used, h * NB + b - 3)
                    src = r[f"cache_mem_{which}"][layer, b].rearrange("(a p) h d -> p a h d", p=P)[:, :, bass.ds(h, 1), :]
                    sp.dma_start(KV[:, b % 4, :].rearrange("p (a o d) -> p a o d", a=2, o=1), src).then_inc(kv_in[b % 4], 16)

                for b in range(NB):
                    cached(b, "k")
                for q, src in enumerate(out_units(w["o"], h * HD)):
                    G.load(sp, h * UNITS + 12 + q, q, src)
                for b in range(NB):
                    cached(b, "v")

            heads(sp, head)
            sp.wait_ge(k_stored, 16 * NH)
            sp.wait_ge(v_stored, 16 * NH)

        @block.gpsimd
        def _(pool):
            G.split_all(pool, UNITS * NH)

        MB = ((0, 1), (2, 6))

        @block.tensor
        def _(pe):
            pe.wait_ge(mem_n, 2)
            for a in range(2):
                for kh in range(2):
                    for k in range(4):
                        mm = pe.transpose(c.PS[:, MB[a][kh], k * P:(k + 1) * P],
                                          MN[:, a, (4 * kh + k) * P:(4 * kh + k + 1) * P], c.ident[:, :])
                    mm.then_inc(mem_turned, 1)

            def memory_tile(h, first, n):
                if first:
                    if n == 0:
                        pe.wait_ge(mt_lo, 4)
                    else:
                        norm.tensor(pe)
                        pe.wait_ge(norm.std, 1)
                else:
                    pe.wait_ge(G.freed[n], h * (TILES // 2))
                for k in range(KD):
                    s = k // 2 % SPLIT
                    if k % 2 == 0:
                        pe.wait_ge(G.w_split, h * UNITS + 4 * n + k // 2 + 1)
                    cols = slice((k % 2) * HD, (k % 2 + 1) * HD)
                    for i, (m, x) in enumerate(((MTh, c.Wh), (MTh, c.Wl), (MTl, c.Wh))):
                        for a in range(2):
                            mm = pe.matmul(group(c, n)[:, a, 0:HD], m[:, k, a * P:(a + 1) * P], x[:, s, cols],
                                           start=k == 0 and i == 0, stop=k == KD - 1 and i == 2)
                    mm.then_inc(G.half, 1)

            def sample_k(h, b):
                pe.wait_ge(kv_in[b % 4], h * 64 + 16 * (b // 4 + 1))
                if b >= 2:
                    pe.wait_ge(ks_copied, h * NB + b - 1)
                for a in range(2):
                    for d in range(2):
                        mm = pe.transpose(c.PS[:, 3 + b % 2, d * MEM + a * P:d * MEM + (a + 1) * P],
                                          KV[:, b % 4, a * HD + d * P:a * HD + (d + 1) * P], c.ident[:, :])
                mm.then_inc(ks_turned, 1)

            def sample_scores(h, b):
                pe.wait_ge(ks_copied, h * NB + b + 1)
                if b == 0:
                    pe.wait_ge(qm_set, h * 2 + 2)
                for d in range(2):
                    mm = pe.matmul(c.PS[0:NS, 5, 0:MEM], QM[:, d, NS * b:NS * (b + 1)], KTS[:, b % 2, d * MEM:(d + 1) * MEM],
                                   start=b == 0 and d == 0, stop=b == NB - 1 and d == 1)
                mm.then_inc(s_scored, 1)

            def scores(h, t):
                if t >= 2:
                    pe.wait_ge(exped, h * NT + t - 1)
                for d in range(2):
                    mm = pe.matmul(c.PS[:, t % 2, 0:MEM], Q[:, d, t * P:(t + 1) * P], KT[:, d, :], start=d == 0, stop=d == 1)
                mm.then_inc(scored, 1)

            def turn(h, t, first):
                pe.wait_ge(weighed, h * NT + t + 1)
                if t >= 2:
                    pe.wait_ge(p_copied, h * NT + t - 1)
                elif not first:
                    pe.wait_ge(s_copied, h)
                for a in range(2):
                    mm = pe.transpose(c.PS[:, 6 + t % 2, a * P:(a + 1) * P], E[:, t % 2, a * P:(a + 1) * P], c.ident[:, :])
                mm.then_inc(p_turned, 1)

            def prompt_o(h, d):
                for q in range(3):
                    lo, hi = q * PART, min((q + 1) * PART, T)
                    if q == 2 and d == 1:
                        pe.wait_ge(s_weighed, h + 1)
                        pe.wait_ge(p_copied, h * NT + NT)
                    for a in range(2):
                        pe.matmul(group(c, d)[:, q, 0:hi - lo], VN[:, a, d * P:(d + 1) * P], PT[:, a, lo:hi],
                                  start=a == 0, stop=a == 1)

            def head(h, first):
                memory_tile(h, first, 0)
                memory_tile(h, first, 1)
                for t in range(2):
                    wait_read(pe, h, t)
                    G.in_tile(pe, h * UNITS + 8 + 2 * t, 2 * t, t, None, norm.lo if first and t == 0 else None)
                    if t == 0:
                        wait_read(pe, h, 0)
                        if not first:
                            pe.wait_ge(p_copied, h * NT)
                            pe.wait_ge(s_copied, h)
                        for d in range(2):
                            for a in range(2):
                                mm = pe.transpose(c.PS[:, 7, d * MEM + a * P:d * MEM + (a + 1) * P],
                                                  KN[:, a, d * P:(d + 1) * P], c.ident[:, :])
                        mm.then_inc(kt_turned, 1)
                wait_read(pe, h, 2)
                wait_read(pe, h, 3)
                pe.wait_ge(kt_copied, h + 1)
                scores(h, 0)
                scores(h, 1)
                sample_k(h, 0)
                for t in range(NT):
                    if t + 1 < NB:
                        sample_k(h, t + 1)
                    sample_scores(h, t)
                    turn(h, t, first)
                    if t + 2 < NT:
                        scores(h, t + 2)
                wait_read(pe, h, 1)
                pe.wait_ge(p_copied, h * NT + NT)
                prompt_o(h, 0)
                pe.wait_ge(s_exped, h + 1)
                prompt_o(h, 1)
                for a in range(2):
                    mm = pe.transpose(c.PS[:, 7, a * NS:(a + 1) * NS], ES[:, a * P:(a + 1) * P], c.ident[0:NS, 0:NS])
                mm.then_inc(s_turned, 1)
                pe.wait_ge(s_copied, h + 1)
                for b in range(NB):
                    pe.wait_ge(kv_in[b % 4], h * 64 + 16 * (b // 4 + 3))
                    lo, hi = b * TS, (b + 1) * TS + (4 if b == NB - 1 else 0)
                    for d in range(2):
                        for a in range(2):
                            mm = pe.matmul(group(c, d)[:, 2, T - 2 * PART + lo:T - 2 * PART + hi],
                                           KV[:, b % 4, a * HD + d * P:a * HD + (d + 1) * P], PTS[:, a, lo:hi],
                                           start=a == 0, stop=a == 1)
                    mm.then_inc(v_used, 1)
                pe.wait_ge(y_lo, h * 2 + 2)
                for k in range(KD):
                    if k % 2 == 0:
                        pe.wait_ge(G.w_split, h * UNITS + 12 + k // 2 + 1)
                    G.pair_tile(pe, k // 2, k % 2, k % 2, h * (TILES // 2) + 2 + k // 2, c.Yh, c.Yl)

            heads(pe, head)

        @block.scalar
        def _(act):
            s = nc.scalar
            act.wait_ge(mem_in, 16)
            for a in range(2):
                s.activation(MTh[:, 4 * a:4 * a + 4, :], MN[:, a, :].rearrange("p (k n) -> p k n", k=4), ACT.Square,
                             accum_out=MS[:, a:a + 1]).then_inc(mem_sq, 1)
            act.wait_ge(mem_sq, 2)
            s.activation(MS, MS, ACT.Sqrt, bias=c.eps[:, 0:1], scale=1.0 / D).then_inc(mem_std, 1)
            for n, (a, kh) in enumerate(((0, 0), (0, 1), (1, 0), (1, 1))):
                act.wait_ge(mem_turned, n + 1)
                for k in range(4):
                    k8 = 4 * kh + k
                    mm = s.activation(MTh[:, k8, a * P:(a + 1) * P], c.PS[:, MB[a][kh], k * P:(k + 1) * P], ACT.Copy,
                                      scale=c.prm[:, k8, ROW_MEM + layer:ROW_MEM + layer + 1])
                mm.then_inc(mt_hi, 1)
            norm.scalar(act)

            def head(h, first):
                for n, (rows, stored, out) in enumerate(((KN, k_stored, r["new_mem_k"]), (VN, v_stored, r["new_mem_v"]))):
                    wait_result(act, h, n)
                    if not first:
                        act.wait_ge(stored, h * 16)
                        if n == 0:
                            act.wait_ge(kt_turned, h)
                        else:
                            act.wait_ge(v_used, h * NB)
                    s.activation(rows[:, :, :], group(c, n)[:, 0:2, 0:HD], ACT.Copy).then_inc(G.freed[n], 1)
                    wait_read(act, h, n)
                    dst = out[layer, 0].rearrange("(a p) h d -> p a h d", p=P)[:, :, bass.ds(h, 1), :]
                    act.dma_start(dst, rows[:, :, :].rearrange("p a (o d) -> p a o d", o=1)).then_inc(stored, 16)
                for t in range(2):
                    wait_result(act, h, 2 + t)
                    if not first and t == 0:
                        act.wait_ge(scored, h * NT)
                    s.activation(parts(Q[:, t, :]), group(c, t)[:, :, 0:PART], ACT.Copy,
                                 scale=HD ** -0.5).then_inc(G.freed[t], 1)
                    if t == 0:
                        act.wait_ge(kt_turned, h + 1)
                        s.activation(KT[:, :, :], c.PS[:, 7, :].rearrange("p (d m) -> p d m", d=2), ACT.Copy).then_inc(kt_copied, 1)

                def copy_turned(t):
                    act.wait_ge(p_turned, h * NT + t + 1)
                    s.activation(PT[:, :, t * P:(t + 1) * P], c.PS[:, 6 + t % 2, 0:2 * P].rearrange("p (a n) -> p a n", a=2),
                                 ACT.Copy).then_inc(p_copied, 1)

                for t in range(NT):
                    if t >= 2 or not first:
                        act.wait_ge(p_turned, h * NT + t - 1)
                    act.wait_ge(maxed, h * NT + t + 1)
                    s.activation(E[:, t % 2, :], c.PS[:, t % 2, 0:MEM], ACT.Exp, bias=NM[:, t % 2:t % 2 + 1],
                                 accum_out=SUM[:, t % 2:t % 2 + 1]).then_inc(exped, 1)
                    if t >= 1:
                        copy_turned(t - 1)
                copy_turned(NT - 1)
                act.wait_ge(s_maxed, h + 1)
                s.activation(ES[:, :], c.PS[0:NS, 5, 0:MEM], ACT.Exp, bias=NMS, accum_out=SUMS).then_inc(s_exped, 1)
                act.wait_ge(s_turned, h + 1)
                s.activation(PTS[:, :, 0:NS], c.PS[:, 7, 0:2 * NS].rearrange("p (a n) -> p a n", a=2), ACT.Copy).then_inc(s_copied, 1)
                act.wait_ge(v_used, h * NB + NB)
                for d in range(2):
                    if not first:
                        act.wait_ge(G.half, h * HALVES)
                    s.activation(parts(c.Yh[:, d, :]), group(c, d)[:, :, 0:PART], ACT.Copy).then_inc(y_hi, 1)

            heads(act, head)

        @block.vector
        def _(dve):
            v = nc.vector
            dve.wait_ge(mem_std, 1)
            v.reciprocal(MS, MS).then_inc(mem_r, 1)
            dve.wait_ge(mem_r, 1)
            for a in range(2):
                v.tensor_scalar(MN[:, a, :], MN[:, a, :], MS[:, a:a + 1], None, ALU.mult).then_inc(mem_n, 1)
            for n, (a, kh) in enumerate(((0, 0), (0, 1), (1, 0), (1, 1))):
                dve.wait_ge(mt_hi, n + 1)
                for k in range(4):
                    k8 = 4 * kh + k
                    mm = v.scalar_tensor_tensor(MTl[:, k8, a * P:(a + 1) * P], c.PS[:, MB[a][kh], k * P:(k + 1) * P],
                                                c.prm[:, k8, ROW_MEM + layer:ROW_MEM + layer + 1],
                                                MTh[:, k8, a * P:(a + 1) * P].bitcast(F32), ALU.mult, ALU.subtract)
                mm.then_inc(mt_lo, 1)
            dve.wait_ge(mem_turned, 4)
            v.memset(QM[:, :, :], 0.0).then_inc(init, 1)
            v.memset(PTS[:, :, NS:NS + 4], 0.0).then_inc(init, 1)
            norm.vector(dve, ROW_X + layer)
            dve.wait_ge(init, 2)

            def head(h, first):
                if not first:
                    dve.wait_ge(s_scored, h * NB)
                for d in range(2):
                    wait_read(dve, h, 2 + d)
                    v.tensor_copy(QM[:, d, :].rearrange("p (b n) -> p b n", b=NB)[:, :, 0:TS],
                                  Q[:, d, T:TA].rearrange("p (b t) -> p b t", b=NB)).then_inc(qm_set, 1)

                def maximum(t):
                    dve.wait_ge(scored, h * NT + t + 1)
                    v.tensor_reduce(NM[:, t % 2:t % 2 + 1], c.PS[:, t % 2, 0:MEM], AX_X, ALU.max, negate=True).then_inc(maxed, 1)

                def sample_k(b):
                    dve.wait_ge(ks_turned, h * NB + b + 1)
                    if b >= 2 or not first:
                        dve.wait_ge(s_scored, h * NB + b - 1)
                    v.tensor_copy(KTS[:, b % 2, :], c.PS[:, 3 + b % 2, :]).then_inc(ks_copied, 1)

                maximum(0)
                sample_k(0)
                for t in range(NT):
                    if t + 1 < NT:
                        maximum(t + 1)
                    i = t % 2
                    dve.wait_ge(exped, h * NT + t + 1)
                    v.reciprocal(SUM[:, i:i + 1], SUM[:, i:i + 1]).then_inc(inverted, 1)
                    dve.wait_ge(inverted, h * NT + t + 1)
                    v.tensor_scalar(E[:, i, :], E[:, i, :], SUM[:, i:i + 1], None, ALU.mult).then_inc(weighed, 1)
                    if t + 1 < NB:
                        sample_k(t + 1)
                dve.wait_ge(s_scored, h * NB + NB)
                v.tensor_reduce(NMS, c.PS[0:NS, 5, 0:MEM], AX_X, ALU.max, negate=True).then_inc(s_maxed, 1)
                dve.wait_ge(s_exped, h + 1)
                v.reciprocal(SUMS, SUMS).then_inc(s_inverted, 1)
                dve.wait_ge(s_inverted, h + 1)
                v.tensor_scalar(ES[:, :], ES[:, :], SUMS, None, ALU.mult).then_inc(s_weighed, 1)
                for d in range(2):
                    dve.wait_ge(y_hi, h * 2 + d + 1)
                    v.tensor_tensor(parts(c.Yl[:, d, :]), group(c, d)[:, :, 0:PART], parts(c.Yh[:, d, :].bitcast(F32)),
                                    ALU.subtract).then_inc(y_lo, 1)
                for k in range(KD):
                    wait_result(dve, h, 4 + k)
                    if not first:
                        dve.wait_ge(G.freed[k % 2], h * (TILES // 2) + 2 + k // 2)
                    v.tensor_tensor(parts(c.X[:, k, :]), group(c, k % 2)[:, :, 0:PART], parts(c.X[:, k, :]),
                                    ALU.add).then_inc(G.freed[k % 2], 1)

            heads(dve, head)


def block_odd(c, name):
    nc, r = c.nc, c.dram
    c.at = c.region
    PAIRS = WC // 256
    w_in, w_out = r["w_in_odd"][0], r["w_out_odd"][0]
    hist_rows = r["state_short"][0].rearrange("b t c -> (b t) c")
    with ExitStack() as ctx:
        sem = semaphores(c, ctx, f"{name}_")
        norm = Norm(c, sem, f"{name}n")
        XV = lay(c, f"{name}_XV", [P, TP])
        U = lay(c, f"{name}_U", [P, HS + TP])
        US = lay(c, f"{name}_US", [P, NB, HS + TS])
        CV = lay(c, f"{name}_CV", [P, 2, TP])
        GS = lay(c, f"{name}_GS", [P, TP])
        SW = lay(c, f"{name}_SW", [P, WC // P, 3])
        TL = lay(c, f"{name}_TL", [P, NB * HS])
        SN = lay(c, f"{name}_SN", [P, P])
        OS = lay(c, f"{name}_OS", [P, 2, P])
        G = Gemm(c, sem)
        hist_in, hist_turned, hist_copied = sem("hist_in"), sem("hist_turned"), sem("hist_copied")
        tail_copied = sem("tail_copied")
        u_turned, rows_copied, rows_stored = sem("u_turned"), sem("rows_copied"), sem("rows_stored")
        init, us_new, cv, y_done, y_hi, y_lo = sem("init"), sem("us_new"), sem("cv"), sem("y_done"), sem("y_hi"), sem("y_lo")
        block = ctx.enter_context(nc.Block())

        def chunk(g, odd):
            if isinstance(g, int) and g == 0:
                return odd, 8 * odd, 4 * odd
            return g * 2 + odd, g * 20 + (8 if odd else -4), g * 16 + (4 if odd else -8)

        def projection(g, last=False):
            return (g * 20 + 24, g * 16 + 12) if not last else (g * 20 + 16, g * 16 + 8)

        def tile_done(u, i):
            return u * 2 + 4 * (i + 1)

        def read(t, i):
            return t_half(t) + i // 2 + 1

        def t_half(t):
            return t // 2

        @block.sync
        def _(sp):
            def load_chunk(g, odd):
                j, u, t = chunk(g, odd)
                if odd or not isinstance(g, int):
                    sp.wait_ge(hist_turned, j)
                sp.dma_start(SN[0:NB * HS, :], hist_rows[:, bass.ds(j * P, P)]).then_inc(hist_in, 16)
                for i, part in enumerate((2, 1, 3, 0)):
                    for h, src in enumerate(in_units(w_in, j * P + part * WC)):
                        n = 2 * i + h
                        G.load(sp, u + n, n, src, wait=odd or n >= RAW or not isinstance(g, int))

            def load_out(g, last=False):
                u, t = projection(g, last)
                for q, src in enumerate(out_units(w_out, g * 256)):
                    G.load(sp, u + q, q, src)

            load_chunk(0, 0)
            load_chunk(0, 1)
            with sp.Fori(1, PAIRS) as g:
                load_chunk(g, 0)
                load_out(g - 1)
                load_chunk(g, 1)
            load_out(PAIRS - 1, True)
            sp.wait_ge(rows_stored, 32 * 2 * PAIRS)

        @block.gpsimd
        def _(pool):
            G.split_all(pool, 20 * PAIRS)

        @block.tensor
        def _(pe):
            def in_chunk(g, odd):
                j, u, t = chunk(g, odd)
                first = isinstance(g, int)
                pe.wait_ge(hist_in, (j + 1) * 16)
                if not first or odd:
                    pe.wait_ge(hist_copied, j)
                for i in range(4):
                    freed = None if first and not odd and i < 2 else t_half(t) + i // 2
                    G.in_tile(pe, u + 2 * i, 2 * i, i % 2, freed, norm.lo if first and not odd and i == 0 else None)
                    if i == 0:
                        pe.transpose(c.PS[:, 6, 0:NB * HS], SN[0:NB * HS, :],
                                     c.ident[0:NB * HS, 0:NB * HS]).then_inc(hist_turned, 1)
                pe.wait_ge(us_new, j + 1)
                pe.wait_ge(tail_copied, j + 1)
                if not first or odd:
                    pe.wait_ge(rows_copied, j * 2)
                pe.transpose(c.PS[0:HS, 7, 0:P], U[:, T:HS + T], c.ident[:, :])
                pe.transpose(c.PS[0:NB * HS, 7, P:2 * P], TL[:, :], c.ident[:, :]).then_inc(u_turned, 1)

            def project(g, last=False):
                u, t = projection(g, last)
                pe.wait_ge(y_lo, g * 2 + 2)
                for k in range(KD):
                    if k % 2 == 0:
                        pe.wait_ge(G.w_split, u + k // 2 + 1)
                    G.pair_tile(pe, k // 2, k % 2, k % 2, t_half(t) + k // 2, c.Yh, c.Yl)

            norm.tensor(pe)
            in_chunk(0, 0)
            in_chunk(0, 1)
            with pe.Fori(1, PAIRS) as g:
                in_chunk(g, 0)
                project(g - 1)
                in_chunk(g, 1)
            project(PAIRS - 1, True)

        @block.scalar
        def _(act):
            def in_chunk(g, odd):
                j, u, t = chunk(g, odd)
                first = isinstance(g, int)
                again = odd or not first
                act.wait_ge(hist_turned, j + 1)
                if again:
                    act.wait_ge(cv, j * 6)
                nc.scalar.activation(US[:, :, 0:HS], c.PS[:, 6, 0:NB * HS].rearrange("p (b t) -> p b t", b=NB),
                                     ACT.Copy).then_inc(hist_copied, 1)
                act.wait_ge(G.half, tile_done(u, 0))
                if again:
                    act.wait_ge(y_done, j)
                nc.scalar.activation(parts(XV[:, :]), group(c, 0)[:, :, 0:PART], ACT.Copy).then_inc(G.freed[0], 1)
                act.wait_ge(G.half, tile_done(u, 2))
                nc.scalar.activation(parts(GS[:, :]), group(c, 0)[:, :, 0:PART], ACT.Silu).then_inc(G.freed[0], 1)
                act.wait_ge(us_new, j + 1)
                act.wait_ge(hist_copied, j + 1)
                nc.scalar.activation(TL[:, :].rearrange("p (b t) -> p b t", b=NB), US[:, :, TS:HS + TS],
                                     ACT.Copy).then_inc(tail_copied, 1)
                act.wait_ge(u_turned, j + 1)
                if again:
                    act.wait_ge(rows_stored, j * 32)
                nc.scalar.activation(OS[0:HS, 0, :], c.PS[0:HS, 7, 0:P], ACT.Copy).then_inc(rows_copied, 1)
                nc.scalar.activation(OS[0:NB * HS, 1, :], c.PS[0:NB * HS, 7, P:2 * P], ACT.Copy).then_inc(rows_copied, 1)
                act.wait_ge(rows_copied, j * 2 + 2)
                cols = bass.ds(j * P, P)
                act.dma_start(r["new_short_prompt"][0, 0, :, cols], OS[0:HS, 0, :]).then_inc(rows_stored, 16)
                act.dma_start(r["new_short_sample"][0].rearrange("b t c -> (b t) c")[:, cols],
                              OS[0:NB * HS, 1, :]).then_inc(rows_stored, 16)
                act.wait_ge(y_done, j + 1)
                if not first:
                    up, tp = projection(g - 1)
                    act.wait_ge(G.half, up * 2 + KD)
                nc.scalar.activation(c.Yh[:, odd, :], CV[:, odd, :], ACT.Copy).then_inc(y_hi, 1)

            norm.scalar(act)
            in_chunk(0, 0)
            in_chunk(0, 1)
            with act.Fori(1, PAIRS) as g:
                in_chunk(g, 0)
                in_chunk(g, 1)

        @block.vector
        def _(dve):
            v = nc.vector

            def in_chunk(g, odd):
                j, u, t = chunk(g, odd)
                first = isinstance(g, int)
                again = odd or not first
                dve.wait_ge(G.half, tile_done(u, 1))
                dve.wait_ge(G.freed[0], read(t, 0))
                if again:
                    dve.wait_ge(u_turned, j)
                    dve.wait_ge(cv, j * 6)
                v.tensor_tensor(parts(U[:, HS:HS + TP]), group(c, 1)[:, :, 0:PART], parts(XV[:, :]),
                                ALU.mult).then_inc(G.freed[1], 1)
                dve.wait_ge(G.freed[1], read(t, 1))
                v.tensor_copy(US[:, :, HS:HS + TS], U[:, HS + T:HS + TA].rearrange("p (b t) -> p b t", b=NB)).then_inc(us_new, 1)
                if not first:
                    dve.wait_ge(y_lo, j - 1)
                dve.wait_ge(us_new, j + 1)
                dve.wait_ge(hist_copied, j + 1)
                outs = (CV[:, odd, 0:T], CV[:, odd, T:TA].rearrange("p (b t) -> p b t", b=NB))
                for n in range(3):
                    ins = (U[:, n:n + T], US[:, :, n:n + TS])
                    tap = SW[:, bass.ds(j, 1), n]
                    for s in range(2):
                        if n == 0:
                            v.tensor_scalar(outs[s], ins[s], tap, None, ALU.mult).then_inc(cv, 1)
                        else:
                            dve.wait_ge(cv, j * 6 + 2 * (n - 1) + s + 1)
                            v.scalar_tensor_tensor(outs[s], ins[s], tap, outs[s], ALU.mult, ALU.add).then_inc(cv, 1)
                dve.wait_ge(cv, j * 6 + 6)
                dve.wait_ge(G.half, tile_done(u, 3))
                v.tensor_tensor(parts(CV[:, odd, :]), group(c, 1)[:, :, 0:PART], parts(CV[:, odd, :]),
                                ALU.mult).then_inc(G.freed[1], 1)
                dve.wait_ge(G.freed[1], read(t, 3))
                dve.wait_ge(G.freed[0], read(t, 2))
                v.tensor_tensor(CV[:, odd, :], CV[:, odd, :], GS[:, :], ALU.mult).then_inc(y_done, 1)

            def low(j, odd):
                dve.wait_ge(y_hi, j + 1)
                v.tensor_tensor(c.Yl[:, odd, :], CV[:, odd, :], c.Yh[:, odd, :].bitcast(F32),
                                ALU.subtract).then_inc(y_lo, 1)

            def add(g, last=False):
                u, t = projection(g, last)
                for k in range(KD):
                    dve.wait_ge(G.half, u * 2 + k + 1)
                    v.tensor_tensor(parts(c.X[:, k, :]), group(c, k % 2)[:, :, 0:PART], parts(c.X[:, k, :]),
                                    ALU.add).then_inc(G.freed[k % 2], 1)
                    dve.wait_ge(G.freed[k % 2], t_half(t) + k // 2 + 1)

            v.memset(U[:, 0:HS], 0.0).then_inc(init, 1)
            v.memset(CV[:, :, TA:TP], 0.0).then_inc(init, 1)
            for n in range(3):
                for h in range(2):
                    v.tensor_copy(SW[:, KD * h:KD * (h + 1), n], c.prm[:, :, ROW_SHORT + 2 * n + h]).then_inc(init, 1)
            norm.vector(dve, ROW_MIX + 1)
            dve.wait_ge(init, 8)
            in_chunk(0, 0)
            low(0, 0)
            in_chunk(0, 1)
            low(1, 1)
            with dve.Fori(1, PAIRS) as g:
                in_chunk(g, 0)
                add(g - 1)
                low(g * 2, 0)
                in_chunk(g, 1)
                low(g * 2 + 1, 1)
            add(PAIRS - 1, True)



def program(nc, dram):
    c = Core()
    c.nc, c.dram = nc, dram
    with ExitStack() as ctx:
        c.PS = ctx.enter_context(nc.psum_tensor("PS", [P, 8, 512], F32))
        place(c)
        block_load(c)
        block_even(c)
        block_cross(c, 0)
        block_odd(c, "odd")
        block_cross(c, 1)
        block_final(c)


_INS = ["x_prompt", "x_sample", "state_pool", "state_conv", "state_short", "cache_mem_k", "cache_mem_v", "mem_prompt",
        "norm_mix", "w_in_even", "pool_w", "pool_scale", "conv_w", "conv_b", "ln_g", "ln_b", "w_out_even",
        "w_in_odd", "short_w", "w_out_odd", "norm_x", "norm_mem", "w_q", "w_k", "w_v", "w_o", "final_norm"]
_OUTS = [("y_prompt", (1, T, D)), ("y_sample", (NB, TS, D)), ("new_pool_prompt", (1, 1, HPOOL, WB)),
         ("new_conv_prompt", (1, 1, HC, WB)), ("new_short_prompt", (1, 1, HS, WC)),
         ("new_mem_k", (2, 1, MEM, NH, HD)), ("new_mem_v", (2, 1, MEM, NH, HD)),
         ("new_pool_sample", (1, NB, HPOOL, WB)), ("new_conv_sample", (1, NB, HC, WB)), ("new_short_sample", (1, NB, HS, WC))]


def kernel(**inputs):
    import numpy as _np
    import concourse.bacc as _bacc
    from concourse import mybir as _mybir
    from concourse.bass_utils import run_bass_kernel_spmd as _run

    nc = _bacc.Bacc("TRN2", target_bir_lowering=False, num_devices=1)
    arrays, dram = {}, {}
    for name in _INS:
        a = _np.ascontiguousarray(inputs[name])
        arrays[f"in_{name}"] = a
        dram[name] = nc.dram_tensor(f"in_{name}", a.shape, _mybir.dt.from_np(a.dtype), kind="ExternalInput").ap()
    for name, shape in _OUTS:
        dram[name] = nc.dram_tensor(f"out_{name}", shape, _mybir.dt.float32, kind="ExternalOutput").ap()
    dram["conv_scratch"] = nc.dram_tensor("conv_scratch", (KD, P, TP), _mybir.dt.float32, kind="Internal").ap()
    program(nc, dram)
    r = _run(nc, [arrays], core_ids=[0])
    return tuple(r.results[0][f"out_{name}"] for name, _ in _OUTS)
```

```python
from contextlib import ExitStack

import concourse.bass as bass
from concourse import mybir

F32 = mybir.dt.float32
F32R = mybir.dt.float32r
ALU = mybir.AluOpType
ACT = mybir.ActivationFunctionType
AX_X = mybir.AxisListType.X

P = 128
D = 1024
KD = D // P
T = 1024
NB, TS = 8, 8
NS = NB * TS
TA = T + NS
PART = 364
TP = 3 * PART
WB = 1024
WC = 2048
CONV = 31
HC = CONV - 1
HPOOL = 15
HS = 2
MEM = 256
NH = 4
HD = 256
EPS = 1e-6
UNIT = 512
RAW, SPLIT = 2, 4

ROW_CONV_W, ROW_MIX, ROW_X, ROW_MEM, ROW_FINAL = 0, 31, 33, 35, 37
ROW_CONV_B, ROW_LN_G, ROW_LN_B, ROW_POOL, ROW_SHORT = 38, 39, 40, 41, 42
ROWS = 48


class Core:
    pass


def place(c):
    nc = c.nc
    c.at = 16512
    c.X = persistent(c, "x_res", [P, KD, TP], F32)
    c.Hh = persistent(c, "h_hi", [P, KD, TP], F32R)
    c.Hl = persistent(c, "h_lo", [P, KD, TP], F32R)
    c.Yh = persistent(c, "y_hi", [P, 2, TP], F32R)
    c.Yl = persistent(c, "y_lo", [P, 2, TP], F32R)
    c.Wraw = persistent(c, "w_raw", [P, RAW, UNIT], F32)
    c.Wh = persistent(c, "w_hi", [P, SPLIT, UNIT], F32R)
    c.Wl = persistent(c, "w_lo", [P, SPLIT, UNIT], F32R)
    c.ident = persistent(c, "ident", [P, P], F32)
    c.ones = persistent(c, "ones", [P, P], F32)
    c.prm = persistent(c, "prm", [P, KD, ROWS], F32)
    c.eps = persistent(c, "eps", [P, 1], F32)
    c.region = c.at
    c.norm_SQ = persistent(c, "norm_SQ", [P, 2, TP], F32)
    c.norm_ACC = persistent(c, "norm_ACC", [P, TP], F32)
    c.norm_R = persistent(c, "norm_R", [P, TP], F32)
    c.norm_ST = persistent(c, "norm_ST", [P, T // P + 1], F32)
    c.norm_end = c.at


def persistent(c, name, shape, dtype):
    size = 4
    for n in shape[1:]:
        size *= n
    t = c.nc.alloc_sbuf_tensor_at(name, shape, dtype, offset=c.at, align_bytes=16)
    c.at += (size + 15) // 16 * 16
    return t


def semaphores(c, ctx, prefix=""):
    given = []

    def sem(name):
        given.append(c.nc.alloc_semaphore(prefix + name))
        return given[-1]

    ctx.callback(c.nc.all_engine_barrier)
    ctx.callback(lambda: c.nc.clear_and_free_semaphores(given))
    return sem


def lay(c, name, shape, dtype=F32):
    return persistent(c, name, shape, dtype)


def group(c, b):
    return c.PS[:, 3 * b:3 * b + 3, :]


def parts(ap):
    return ap.rearrange("p (a n) -> p a n", a=3)


class Gemm:

    def __init__(self, c, sem):
        self.c = c
        self.raw_in = [sem(f"raw_in{i}") for i in range(RAW)]
        self.w_hi = sem("w_hi")
        self.w_split = sem("w_split")
        self.half = sem("half")
        self.freed = [sem(f"freed{i}") for i in range(2)]

    def load(self, sp, u, slot, src, wait=True):
        if wait:
            sp.wait_ge(self.w_split, u - RAW + 1)
        sp.dma_start(self.c.Wraw[:, slot % RAW, :].rearrange("p (a n) -> p a n", n=src.shape[-1]),
                     src).then_inc(self.raw_in[slot % RAW], 16)

    def split_one(self, pool, raw_count, u, s, used):
        c = self.c
        pool.wait_ge(self.raw_in[s % RAW], raw_count)
        if used is not None:
            pool.wait_ge(self.half, used)
        by_128 = lambda ap: ap.rearrange("p (a n) -> p a n", n=P)
        ones = c.ones[:, :].unsqueeze(1).to_broadcast([P, UNIT // P, P])
        c.nc.gpsimd.tensor_tensor(by_128(c.Wh[:, s, :]), by_128(c.Wraw[:, s % RAW, :]), ones,
                                  ALU.mult).then_inc(self.w_hi, 1)
        pool.wait_ge(self.w_hi, u + 1)
        c.nc.gpsimd.tensor_tensor(c.Wl[:, s, :], c.Wraw[:, s % RAW, :], c.Wh[:, s, :].bitcast(F32),
                                  ALU.subtract).then_inc(self.w_split, 1)

    def split_all(self, pool, units):
        for s in range(SPLIT):
            self.split_one(pool, 16 * (s // RAW + 1), s, s, None)
        with pool.Fori(1, units // SPLIT) as i:
            for s in range(SPLIT):
                self.split_one(pool, i * 32 + 16 * (s // RAW + 1), i * SPLIT + s, s, i * 8 + 2 * s - 6)

    def in_tile(self, pe, u, slot, b, freed, k_ready=None):
        c = self.c
        ps = group(c, b)
        if freed is not None:
            pe.wait_ge(self.freed[b], freed)
        for k in range(KD):
            s = (slot + k // 4) % SPLIT
            if k % 4 == 0:
                pe.wait_ge(self.w_split, u + k // 4 + 1)
            if k_ready is not None:
                pe.wait_ge(k_ready, k + 1)
            cols = slice(P * (k % 4), P * (k % 4 + 1))
            three_passes(pe, ps, c.Wh[:, s, cols], c.Wl[:, s, cols], c.Hh[:, k, :], c.Hl[:, k, :],
                         k == 0, k == KD - 1, self.half if k % 2 else None)

    def first_tiles(self, pe, k_ready, u=0):
        c = self.c
        for k in range(KD):
            pe.wait_ge(k_ready, k + 1)
            for b in range(2):
                s = 2 * (k // 4) + b
                if k % 4 == 0:
                    pe.wait_ge(self.w_split, u + s + 1)
                cols = slice(P * (k % 4), P * (k % 4 + 1))
                three_passes(pe, group(c, b), c.Wh[:, s, cols], c.Wl[:, s, cols], c.Hh[:, k, :], c.Hl[:, k, :],
                             k == 0, k == KD - 1, self.half if k % 4 == 3 else None, 2)

    def pair_tile(self, pe, slot, e, b, freed, Ah, Al, second=None):
        c = self.c
        if freed is not None:
            pe.wait_ge(self.freed[b], freed)
        s = slot % SPLIT
        for k in range(2):
            if k and second is not None:
                pe.wait_ge(*second)
            cols = slice(256 * k + P * e, 256 * k + P * (e + 1))
            three_passes(pe, group(c, b), c.Wh[:, s, cols], c.Wl[:, s, cols], Ah[:, k, :], Al[:, k, :],
                         k == 0, k == 1, self.half if k else None)


def three_passes(pe, ps, wh, wl, ah, al, first, last, signal, count=1):
    for w, a, n in ((wh, ah, 0), (wh, al, 1), (wl, ah, 2)):
        for q in range(3):
            mm = pe.matmul(ps[:, q, 0:PART], w, a[:, q * PART:(q + 1) * PART],
                           start=first and n == 0, stop=last and n == 2)
    if signal is not None:
        mm.then_inc(signal, count)


def first_units(w, col0, col1):
    (a, b), (d, e) = in_units(w, col0), in_units(w, col1)
    return [a, d, b, e]


def in_units(w, col):
    v = w.rearrange("(h k p) n -> h p k n", h=2, p=P)
    return [v[h, :, :, bass.ds(col, P)] for h in range(2)]


def out_units(w, row):
    return [w[bass.ds(row, 256), 256 * q:256 * (q + 1)].rearrange("(k p) n -> p k n", p=P) for q in range(4)]


class Norm:
    TILES = T // P + 1
    START = [P * t for t in range(T // P)] + [TP - P]

    def __init__(self, c, sem, b=1, summed=True):
        self.c, self.b, self.summed = c, b, summed
        self.next_sq, self.next_acc = sem("next_sq"), sem("next_acc")
        self.sq, self.acc = sem("norm_sq"), sem("norm_acc")
        self.sum, self.std, self.inv = sem("norm_sum"), sem("norm_std"), sem("norm_inv")
        self.diag, self.spread, self.rstd = sem("norm_diag"), sem("norm_spread"), sem("norm_rstd")
        self.t, self.hi, self.lo = sem("norm_t"), sem("norm_hi"), sem("norm_lo")
        self.SQ, self.ACC, self.R, self.ST = c.norm_SQ, c.norm_ACC, c.norm_R, c.norm_ST
        c.at = c.norm_end
        self.DG = self.SQ[:, :, :].rearrange("p a n -> p (a n)")[:, 0:self.TILES * P]

    def scalar_std(self, act):
        c = self.c
        for k in range(0 if not self.summed else KD, KD):
            if k >= 2:
                act.wait_ge(self.acc, max(1, k - 2))
            c.nc.scalar.activation(self.SQ[:, k % 2, :], c.X[:, k, :], ACT.Square).then_inc(self.sq, 1)
        act.wait_ge(self.sum, 1)
        sums = group(c, self.b)[:, 2, 400:400 + 4 * self.TILES].rearrange("p (t n) -> p t n", n=4)[:, :, 0]
        c.nc.scalar.activation(self.ST[:, :], sums, ACT.Sqrt, bias=c.eps[:, 0:1], scale=1.0 / D).then_inc(self.std, 1)
        act.wait_ge(self.spread, 2)
        c.nc.scalar.activation(self.R[:, 0:6 * P].rearrange("p (a n) -> p a n", a=2),
                               group(c, self.b)[:, 0:2, 0:3 * P], ACT.Copy).then_inc(self.rstd, 1)
        act.wait_ge(self.spread, 3)
        c.nc.scalar.activation(self.R[:, 6 * P:TP], group(c, self.b)[:, 2, 0:TP - 6 * P], ACT.Copy).then_inc(self.rstd, 1)

    def next_squares(self, act, wait_chunk):
        for k in range(KD):
            wait_chunk(k)
            if k >= 2:
                act.wait_ge(self.next_acc, max(1, k - 2))
            self.c.nc.scalar.activation(self.SQ[:, k % 2, :], self.c.X[:, k, :], ACT.Square).then_inc(self.next_sq, 1)

    def next_sums(self, pool):
        tt = self.c.nc.gpsimd.tensor_tensor
        pool.wait_ge(self.next_sq, 2)
        tt(self.ACC[:, :], self.SQ[:, 0, :], self.SQ[:, 1, :], ALU.add).then_inc(self.next_acc, 1)
        for k in range(2, KD):
            pool.wait_ge(self.next_sq, k + 1)
            pool.wait_ge(self.next_acc, k - 1)
            tt(self.ACC[:, :], self.ACC[:, :], self.SQ[:, k % 2, :], ALU.add).then_inc(self.next_acc, 1)

    def scalar_split(self, act, first=0, last=KD):
        c = self.c
        for k in range(first, last):
            act.wait_ge(self.t, k + 1)
            c.nc.scalar.activation(c.Hh[:, k, :], self.SQ[:, k % 2, :], ACT.Copy).then_inc(self.hi, 1)

    def scalar(self, act):
        self.scalar_std(act)
        self.scalar_split(act)

    def tensor(self, pe):
        if not self.summed:
            pe.wait_ge(self.acc, KD - 1)
        ps = group(self.c, self.b)
        for t, at in enumerate(self.START):
            mm = pe.matmul(ps[:, 2, 400 + 4 * t:404 + 4 * t], self.ACC[:, at:at + P], self.c.ones[:, 0:4], start=True, stop=True)
        mm.then_inc(self.sum, 1)
        for q in range(3):
            pe.wait_ge(self.diag, q + 1)
            n = 3 * P if q < 2 else 2 * P
            mm = pe.matmul(ps[:, q, 0:n], self.c.ones[:, :], self.DG[:, 3 * P * q:3 * P * q + n], start=True, stop=True)
            if q == 2:
                mm = pe.matmul(ps[:, q, n:TP - 6 * P], self.c.ones[:, :], self.DG[:, 9 * P - (TP - T):9 * P],
                               start=True, stop=True)
            mm.then_inc(self.spread, 1)

    def vector_rstd(self, dve):
        c = self.c
        if not self.summed:
            dve.wait_ge(self.sq, 2)
            c.nc.vector.tensor_tensor(self.ACC[:, :], self.SQ[:, 0, :], self.SQ[:, 1, :], ALU.add).then_inc(self.acc, 1)
            for k in range(2, KD):
                dve.wait_ge(self.sq, k + 1)
                dve.wait_ge(self.acc, k - 1)
                c.nc.vector.tensor_tensor(self.ACC[:, :], self.ACC[:, :], self.SQ[:, k % 2, :],
                                          ALU.add).then_inc(self.acc, 1)
        dve.wait_ge(self.std, 1)
        c.nc.vector.reciprocal(self.ST[:, :], self.ST[:, :]).then_inc(self.inv, 1)
        dve.wait_ge(self.inv, 1)
        if not self.summed:
            dve.wait_ge(self.acc, KD - 1)
        for q in range(3):
            c.nc.vector.tensor_tensor(self.DG[:, 3 * P * q:3 * P * (q + 1)].rearrange("p (t n) -> p t n", n=P),
                                      c.ident[:, :].unsqueeze(1).to_broadcast([P, 3, P]),
                                      self.ST[:, 3 * q:3 * q + 3].unsqueeze(2).to_broadcast([P, 3, P]),
                                      ALU.mult).then_inc(self.diag, 1)
        dve.wait_ge(self.rstd, 2)

    def vector(self, dve, row):
        self.vector_rstd(dve)
        self.vector_split(dve, row)

    def vector_split(self, dve, row):
        c = self.c

        def low(k):
            dve.wait_ge(self.hi, k + 1)
            c.nc.vector.tensor_tensor(c.Hl[:, k, :], self.SQ[:, k % 2, :], c.Hh[:, k, :].bitcast(F32),
                                      ALU.subtract).then_inc(self.lo, 1)

        for k in range(KD):
            if k >= 2:
                dve.wait_ge(self.lo, k - 1)
            c.nc.vector.scalar_tensor_tensor(self.SQ[:, k % 2, :], c.X[:, k, :], c.prm[:, k, row:row + 1],
                                             self.R[:, :], ALU.mult, ALU.mult).then_inc(self.t, 1)
            if k >= 1:
                low(k - 1)
        low(KD - 1)


def block_load(c):
    nc = c.nc
    c.at = c.region
    PR = lay(c, "prm_rows", [P, D])
    XN = lay(c, "x_rows", [P, T // P + 1, D])
    with ExitStack() as ctx:
        sem = semaphores(c, ctx)
        prm_in, ident_zero, ident_made, const_made = sem("prm_in"), sem("ident_zero"), sem("ident_made"), sem("const_made")
        x_in = [sem(f"x_in{i}") for i in range(T // P + 1)]
        turned = sem("x_turned")
        copied = [sem("x_copied0"), sem("x_copied1")]
        rows_copied = sem("prm_copied")
        block = ctx.enter_context(nc.Block())
        tiles = T // P + 1

        @block.sync
        def _(sp):
            r = c.dram
            for row, n, ap in ((ROW_CONV_W, CONV, r["conv_w"][0]), (ROW_MIX, 2, r["norm_mix"]), (ROW_X, 2, r["norm_x"]),
                               (ROW_MEM, 2, r["norm_mem"]), (ROW_FINAL, 1, r["final_norm"].rearrange("(a d) -> a d", a=1)),
                               (ROW_CONV_B, 1, r["conv_b"]), (ROW_LN_G, 1, r["ln_g"]), (ROW_LN_B, 1, r["ln_b"]),
                               (ROW_POOL, 1, r["pool_scale"]),
                               (ROW_SHORT, 6, r["short_w"][0].rearrange("t (h d) -> (t h) d", h=2))):
                sp.dma_start(PR[row:row + n, :], ap).then_inc(prm_in, 16)
            for t in range(tiles):
                if t < T // P:
                    sp.dma_start(XN[:, t, :], r["x_prompt"][0, t * P:(t + 1) * P, :]).then_inc(x_in[t], 16)
                else:
                    sp.dma_start(XN[0:NS, t, :], r["x_sample"].rearrange("b t d -> (b t) d")).then_inc(x_in[t], 16)

        @block.gpsimd
        def _(pool):
            nc.gpsimd.memset(c.ident[:, :], 0.0).then_inc(ident_zero, 1)
            pool.wait_ge(ident_zero, 1)
            nc.gpsimd.affine_select(out=c.ident[:, :], in_=c.ident[:, :], compare_op=ALU.not_equal, fill=1.0,
                                    base=0, pattern=[[-1, P]], channel_multiplier=1).then_inc(ident_made, 1)

        @block.tensor
        def _(pe):
            pe.wait_ge(ident_made, 1)
            pe.wait_ge(prm_in, 160)
            for h in range(2):
                for k in range(4):
                    mm = pe.transpose(c.PS[:, h, k * ROWS:(k + 1) * ROWS], PR[0:ROWS, (4 * h + k) * P:(4 * h + k + 1) * P],
                                      c.ident[0:ROWS, 0:ROWS])
                mm.then_inc(turned, 1)
            for t in range(tiles):
                n = P if t < T // P else NS
                pe.wait_ge(x_in[t], 16)
                for h in range(2):
                    if t >= 2:
                        pe.wait_ge(copied[h], t - 1)
                    for k in range(4):
                        mm = pe.transpose(c.PS[:, 2 + 2 * (t % 2) + h, k * P:k * P + n],
                                          XN[0:n, t, (4 * h + k) * P:(4 * h + k + 1) * P], c.ident[0:n, 0:n])
                    mm.then_inc(turned, 1)

        @block.scalar
        def _(act):
            for t in range(tiles):
                n = P if t < T // P else NS
                act.wait_ge(turned, 2 + 2 * t + 1)
                src = c.PS[:, 2 + 2 * (t % 2), :].rearrange("p (k n) -> p k n", k=4)[:, :, 0:n]
                nc.scalar.activation(c.X[:, 0:4, t * P:t * P + n], src, ACT.Copy).then_inc(copied[0], 1)

        @block.vector
        def _(dve):
            nc.vector.memset(c.ones[:, :], 1.0).then_inc(const_made, 1)
            nc.vector.memset(c.eps[:, :], EPS).then_inc(const_made, 1)
            nc.vector.memset(c.X[:, :, TA:TP], 0.0).then_inc(const_made, 1)
            for h in range(2):
                dve.wait_ge(turned, h + 1)
                nc.vector.tensor_copy(c.prm[:, 4 * h:4 * h + 4, :],
                                      c.PS[:, h, 0:4 * ROWS].rearrange("p (k n) -> p k n", k=4)).then_inc(rows_copied, 1)
            for t in range(tiles):
                n = P if t < T // P else NS
                dve.wait_ge(turned, 2 + 2 * t + 2)
                src = c.PS[:, 3 + 2 * (t % 2), :].rearrange("p (k n) -> p k n", k=4)[:, :, 0:n]
                nc.vector.tensor_copy(c.X[:, 4:8, t * P:t * P + n], src).then_inc(copied[1], 1)


def block_final(c):
    nc = c.nc
    c.at = c.region
    tiles = T // P + 1
    THIRD = 3 * P
    with ExitStack() as ctx:
        sem = semaphores(c, ctx)
        norm = Norm(c, sem)
        YN = lay(c, "y_rows", [P, T // P + 1, D])
        scaled, turned, stored = sem("scaled"), sem("y_turned"), sem("y_stored")
        copied = [sem("y_copied0"), sem("y_copied1")]
        block = ctx.enter_context(nc.Block())

        @block.scalar
        def _(act):
            norm.scalar_std(act)
            for t in range(tiles):
                n = P if t < T // P else NS
                act.wait_ge(turned, 2 * t + 1)
                nc.scalar.activation(YN[0:n, t, 0:512], c.PS[0:n, 2 * (t % 2), :], ACT.Copy).then_inc(copied[0], 1)

        @block.tensor
        def _(pe):
            norm.tensor(pe)
            pe.wait_ge(norm.rstd, 2)
            for t in range(tiles):
                n = P if t < T // P else NS
                if t % 3 == 0:
                    pe.wait_ge(scaled, KD * (t // 3 + 1))
                for h in range(2):
                    if t >= 2:
                        pe.wait_ge(copied[h], t - 1)
                    for k in range(4):
                        mm = pe.transpose(c.PS[0:n, 2 * (t % 2) + h, k * P:(k + 1) * P],
                                          c.X[:, 4 * h + k, t * P:t * P + n], c.ident[:, :])
                    mm.then_inc(turned, 1)

        @block.vector
        def _(dve):
            norm.vector_rstd(dve)

            def copy(t):
                n = P if t < T // P else NS
                dve.wait_ge(turned, 2 * t + 2)
                nc.vector.tensor_copy(YN[0:n, t, 512:1024], c.PS[0:n, 2 * (t % 2) + 1, :]).then_inc(copied[1], 1)

            for third in range(3):
                lo, hi = third * THIRD, min((third + 1) * THIRD, TP)
                for k in range(KD):
                    nc.vector.scalar_tensor_tensor(c.X[:, k, lo:hi], c.X[:, k, lo:hi], c.prm[:, k, ROW_FINAL:ROW_FINAL + 1],
                                                   norm.R[:, lo:hi], ALU.mult, ALU.mult).then_inc(scaled, 1)
                if third:
                    for t in range(3 * third - 3, 3 * third):
                        copy(t)
            for t in range(6, tiles):
                copy(t)

        @block.sync
        def _(sp):
            for t in range(tiles):
                sp.wait_ge(copied[0], t + 1)
                sp.wait_ge(copied[1], t + 1)
                if t < T // P:
                    sp.dma_start(c.dram["y_prompt"][0, t * P:(t + 1) * P, :], YN[:, t, :]).then_inc(stored, 16)
                else:
                    sp.dma_start(c.dram["y_sample"].rearrange("b t d -> (b t) d"), YN[0:NS, t, :]).then_inc(stored, 16)
            sp.wait_ge(stored, 16 * tiles)
def even_plan():
    order = []
    for g in range(4):
        order += [(n, 2 * g) for n in ("glu", "val", "ain", "agate")]
        if g:
            order += [("outa", g - 1, k) for k in range(KD)]
        order += [(n, 2 * g + 1) for n in ("glu", "val", "ain", "agate")]
        order += [("pool", 2 * g), ("pool", 2 * g + 1)]
    order += [("bgate", 0), ("bgate", 1)]
    order += [("sum", 0), ("sum", 1)]
    order += [("outa", 3, k) for k in range(KD)]
    for g in range(4):
        if g < 3:
            order += [("bgate", 2 * g + 2), ("bgate", 2 * g + 3)]
        order += [("outb", g, k) for k in range(KD)]
    number, end, half = {}, {}, 0
    for n, tile in enumerate(order):
        half += {"outa": 1, "outb": 1, "pool": 1, "sum": 0}.get(tile[0], 4)
        number[tile], end[tile] = n, half
    end[order[0]] = 6
    return order, number, end


def block_even(c):
    nc, r = c.nc, c.dram
    c.at = c.region
    order, number, end = even_plan()
    w_in, w_out = r["w_in_even"][0], r["w_out_even"][0]
    conv_rows = r["state_conv"][0].rearrange("b t c -> (b t) c")
    pool_rows = r["state_pool"][0].rearrange("b t c -> (b t) c")
    new_conv = r["new_conv_sample"][0].rearrange("b t c -> (b t) c")
    new_pool = r["new_pool_sample"][0].rearrange("b t c -> (b t) c")
    CR, PR = NB * HC // 2, NB * HPOOL
    scratch = r["conv_scratch"]
    TAPS = 2 * CONV
    with ExitStack() as ctx:
        sem = semaphores(c, ctx, f"e_")
        norm = Norm(c, sem, summed=False)
        c.at = c.region
        V = lay(c, "e_V", [P, HC + TP])
        SG = lay(c, "e_SG", [P, TP])
        GS = lay(c, "e_GS", [P, 2, TP])
        A = lay(c, "e_A", [P, HPOOL + TP])
        PT = lay(c, "e_P", [P, TP])
        CB = lay(c, "e_C", [P, 2, TP])
        S1 = lay(c, "e_S1", [P, TP])
        S2 = lay(c, "e_S2", [P, TP])
        Mh = lay(c, "e_Mh", [P, 2, TP], F32R)
        Ml = lay(c, "e_Ml", [P, 2, TP], F32R)
        VS = lay(c, "e_VS", [P, NB, HC + TS])
        AS = lay(c, "e_AS", [P, NB, HPOOL + TS])
        HN = lay(c, "e_HN", [P, 3, P])
        OS = lay(c, "e_OS", [P, 5, P])
        AT = SG[:, 0:184].rearrange("p (b t) -> p b t", b=NB)
        TC = SG[:, 184:424]
        TA_ = SG[:, 424:544]
        G = Gemm(c, sem)
        hist_in, hist_turned, hist_copied = sem("hist_in"), sem("hist_turned"), sem("hist_copied")
        vs_new, as_new, tail_side = sem("vs_new"), sem("as_new"), sem("tail_side")
        tails_turned, rows_copied, rows_stored = sem("tails_turned"), sem("rows_copied"), sem("rows_stored")
        cv, stats, squared, stored = sem("cv"), sem("stats"), sem("squared"), [sem("c_stored0"), sem("c_stored1")]
        level, m_done, m_hi, m_lo, y_hi, y_lo = sem("level"), sem("m_done"), sem("m_hi"), sem("m_lo"), sem("y_hi"), sem("y_lo")
        init, ln_sum, ln_sq, ln_var, ln_std, ln_r = sem("init"), sem("ln_sum"), sem("ln_sq"), sem("ln_var"), sem("ln_std"), sem("ln_r")
        c_in, centred, ln_x, ln_y, yb = [sem("c_in0"), sem("c_in1")], sem("centred"), sem("ln_x"), sem("ln_y"), sem("yb")
        block = ctx.enter_context(nc.Block())

        def bank(tile):
            return group(c, number[tile] % 2)[:, :, 0:PART]

        def wait_result(e, tile):
            e.wait_ge(G.half, end[tile])

        def freed(tile):
            return G.freed[number[tile] % 2]

        def wait_read(e, tile):
            e.wait_ge(freed(tile), number[tile] // 2 + 1)

        @block.sync
        def _(sp):
            u = 0
            for tile in order:
                kind, j = tile[0], tile[1]
                if kind == "glu":
                    if j:
                        sp.wait_ge(hist_turned, j)
                    cols = slice(j * P, (j + 1) * P)
                    sp.dma_start(HN[0:CR, 0:2, :], conv_rows[:, cols].rearrange("(h p) c -> p h c", h=2)).then_inc(hist_in, 16)
                    sp.dma_start(HN[0:PR, 2, :], pool_rows[:, cols]).then_inc(hist_in, 16)
                if kind in ("glu", "val", "ain", "agate", "bgate"):
                    part = {"ain": 0, "agate": 1, "val": 2, "glu": 3, "bgate": 4}[kind]
                    cols = part * WB + j * P
                    if tile == ("val", 0):
                        continue
                    for src in first_units(w_in, cols, 2 * WB) if u == 0 else in_units(w_in, cols):
                        G.load(sp, u, u, src, wait=u >= RAW)
                        u += 1
                elif kind == "pool" and j % 2 == 0:
                    G.load(sp, u, u, r["pool_w"][0, j // 2].rearrange("(k p) n -> p k n", p=P))
                    u += 1
                elif kind in ("outa", "outb") and tile[2] == 0:
                    for src in out_units(w_out, (WB if kind == "outb" else 0) + 256 * j):
                        G.load(sp, u, u, src)
                        u += 1
                if kind == "outa" and j == 3 and tile[2] == 0 or kind == "outb" and tile[2] == 0 and j < 3:
                    for n in (0, 1) if kind == "outa" else (2 * j + 2, 2 * j + 3):
                        if n < 2:
                            sp.wait_ge(stored[n], 16 * KD // 2)
                            sp.wait_ge(stats, 3 * (7 + n))
                        else:
                            sp.wait_ge(yb, n - 1)
                        sp.dma_start(CB[:, n % 2, :], scratch[n]).then_inc(c_in[n % 2], 16)
            sp.wait_ge(rows_stored, 80 * KD)

        @block.gpsimd
        def _(pool):
            G.split_all(pool, 116)
            norm.next_sums(pool)

        @block.tensor
        def _(pe):
            def tails(j):
                pe.wait_ge(tail_side, 2 * (j + 1))
                pe.wait_ge(hist_copied, 2 * (j + 1))
                if j:
                    pe.wait_ge(rows_copied, 5 * j)
                out = c.PS[:, 7, :].rearrange("p (n m) -> p n m", n=4)
                pe.transpose(out[0:HC, 0, :], V[:, T:T + HC], c.ident[:, :])
                pe.transpose(out[0:CR, 1, :], TC[:, 0:CR], c.ident[:, :])
                pe.transpose(out[0:CR, 2, :], TC[:, CR:2 * CR], c.ident[:, :])
                pe.transpose(out[0:HPOOL, 3, :], A[:, T:T + HPOOL], c.ident[:, :])
                pe.transpose(c.PS[0:PR, 6, 384:512], TA_, c.ident[:, :]).then_inc(tails_turned, 1)

            def history(j):
                pe.wait_ge(hist_in, 32 * (j + 1))
                if j:
                    pe.wait_ge(hist_copied, 2 * j)
                if j >= 2:
                    pe.wait_ge(rows_copied, 5 * (j - 1))
                for h in range(3):
                    mm = pe.transpose(c.PS[:, 6, h * CR:(h + 1) * CR], HN[0:CR, h, :], c.ident[0:CR, 0:CR])
                mm.then_inc(hist_turned, 1)

            norm.tensor(pe)
            u = 0
            for tile in order:
                kind, j, n = tile[0], tile[1], number[tile]
                before = n // 2 if n >= 2 else None
                if kind in ("glu", "val", "ain", "agate", "bgate"):
                    if n == 0:
                        pe.wait_ge(norm.rstd, 2)
                        G.first_tiles(pe, norm.lo)
                    elif n > 1:
                        G.in_tile(pe, u, u, n % 2, before)
                    u += 2
                    if kind == "glu":
                        history(j)
                        if j:
                            tails(j - 1)
                    if tile == ("bgate", 0):
                        tails(KD - 1)
                elif kind == "sum":
                    pe.wait_ge(stats, 3 * KD)
                    pe.wait_ge(freed(tile), before)
                    for q in range(3):
                        mm = pe.matmul(group(c, n % 2)[:, q, 0:PART], c.ones[:, :],
                                       (S1, S2)[j][:, q * PART:(q + 1) * PART], start=True, stop=True)
                    mm.then_inc(ln_sum, 1)
                else:
                    k = j % 2 if kind == "pool" else tile[2]
                    if kind == "pool":
                        pe.wait_ge(m_lo, j + 1 + (1 - k))
                    else:
                        pe.wait_ge(y_lo, 2 * j + 2 + (KD if kind == "outb" else 0))
                    if k % 2 == 0:
                        pe.wait_ge(G.w_split, u + 1)
                    Ah, Al = (Mh, Ml) if kind == "pool" else (c.Yh, c.Yl)
                    G.pair_tile(pe, u, k % 2, n % 2, before, Ah, Al)
                    u += k % 2

        @block.scalar
        def _(act):
            s = nc.scalar

            def evacuate(tile, out, func, **more):
                wait_result(act, tile)
                s.activation(parts(out), bank(tile), func, **more).then_inc(freed(tile), 1)

            def store_conv(j):
                act.wait_ge(cv, TAPS * (j + 1))
                act.dma_start(scratch[j], CB[:, j % 2, :]).then_inc(stored[j % 2], 16)
                if j:
                    act.wait_ge(stats, 3 * j)
                s.activation((PT, S2)[j == 0][:, :], CB[:, j % 2, :], ACT.Square).then_inc(squared, 1)

            def history(j):
                act.wait_ge(hist_turned, j + 1)
                s.activation(VS[:, :, 0:HC], c.PS[:, 6, 0:NB * HC].rearrange("p (b t) -> p b t", b=NB),
                             ACT.Copy).then_inc(hist_copied, 1)
                s.activation(AS[:, :, 0:HPOOL], c.PS[:, 6, 2 * CR:2 * CR + PR].rearrange("p (b t) -> p b t", b=NB),
                             ACT.Copy).then_inc(hist_copied, 1)

            def conv_tail(j):
                act.wait_ge(vs_new, j + 1)
                act.wait_ge(hist_copied, 2 * j + 2)
                s.activation(TC.rearrange("p (b t) -> p b t", b=NB), VS[:, :, TS:HC + TS], ACT.Copy).then_inc(tail_side, 1)

            def pool_tail(j):
                act.wait_ge(as_new, j + 1)
                s.activation(TA_.rearrange("p (b t) -> p b t", b=NB), AS[:, :, TS:HPOOL + TS], ACT.Copy).then_inc(tail_side, 1)

            def store_tails(j):
                act.wait_ge(tails_turned, j + 1)
                if j:
                    act.wait_ge(rows_stored, 80 * j)
                for n, rows in enumerate((HC, CR, CR, HPOOL)):
                    s.activation(OS[0:rows, n, :], c.PS[0:rows, 7, n * P:(n + 1) * P], ACT.Copy).then_inc(rows_copied, 1)
                s.activation(OS[0:PR, 4, :], c.PS[0:PR, 6, 384:512], ACT.Copy).then_inc(rows_copied, 1)
                act.wait_ge(rows_copied, 5 * (j + 1))
                cols = slice(j * P, (j + 1) * P)
                act.dma_start(r["new_conv_prompt"][0, 0, :, cols], OS[0:HC, 0, :]).then_inc(rows_stored, 16)
                act.dma_start(new_conv[0:CR, cols], OS[0:CR, 1, :]).then_inc(rows_stored, 16)
                act.dma_start(new_conv[CR:2 * CR, cols], OS[0:CR, 2, :]).then_inc(rows_stored, 16)
                act.dma_start(r["new_pool_prompt"][0, 0, :, cols], OS[0:HPOOL, 3, :]).then_inc(rows_stored, 16)
                act.dma_start(new_pool[:, cols], OS[0:PR, 4, :]).then_inc(rows_stored, 16)

            def pooled_high(j):
                act.wait_ge(m_done, j + 1)
                if j >= 2:
                    wait_result(act, ("pool", 2 * (j // 2) - 1))
                s.activation(Mh[:, j % 2, :], PT[:, :], ACT.Copy).then_inc(m_hi, 1)

            def ya_high(j):
                wait_read(act, ("pool", j))
                if j >= 2:
                    wait_result(act, ("outa", j // 2 - 1, KD - 1))
                s.activation(c.Yh[:, j % 2, :], PT[:, :], ACT.Copy).then_inc(y_hi, 1)

            norm.scalar(act)
            for j in range(KD):
                if j % 2 == 0 and j:
                    ya_high(j - 2)
                    ya_high(j - 1)
                if j:
                    store_tails(j - 1)
                evacuate(("glu", j), SG[:, :], ACT.Sigmoid)
                if j:
                    store_conv(j - 1)
                history(j)
                conv_tail(j)
                if j:
                    act.wait_ge(m_lo, j)
                evacuate(("ain", j), A[:, HPOOL:HPOOL + TP], ACT.Copy)
                pool_tail(j)
                pooled_high(j)
                if j >= 2:
                    wait_read(act, ("pool", j - 2))
                evacuate(("agate", j), GS[:, j % 2, :], ACT.Silu)
            ya_high(KD - 2)
            ya_high(KD - 1)

            def yb_high(j):
                act.wait_ge(yb, j + 1)
                wait_result(act, ("outb", j // 2 - 1, KD - 1) if j >= 2 else ("outa", 3, KD - 1))
                s.activation(c.Yh[:, j % 2, :], PT[:, :], ACT.Copy).then_inc(y_hi, 1)

            def swish(j):
                act.wait_ge(ln_x, j + 1)
                s.activation(CB[:, j % 2, :], CB[:, j % 2, :], ACT.Silu, bias=c.prm[:, j, ROW_LN_B:ROW_LN_B + 1],
                             scale=c.prm[:, j, ROW_LN_G:ROW_LN_G + 1]).then_inc(ln_y, 1)

            for j in range(2):
                wait_read(act, ("pool", KD - 2 + j))
                evacuate(("bgate", j), GS[:, j, :], ACT.Silu)
                if j == 0:
                    store_tails(KD - 1)
            store_conv(KD - 1)
            act.wait_ge(ln_sum, 1)
            s.activation(parts(SG[:, :]), bank(("sum", 0)), ACT.Copy, scale=1.0 / WB).then_inc(freed(("sum", 0)), 1)
            act.wait_ge(ln_var, 1)
            s.activation(V[:, 0:TP], V[:, 0:TP], ACT.Sqrt, bias=c.eps[:, 0:1]).then_inc(ln_std, 1)
            swish(0)
            swish(1)
            for g in range(4):
                yb_high(2 * g)
                yb_high(2 * g + 1)
                if g < 3:
                    for j in (2 * g + 2, 2 * g + 3):
                        evacuate(("bgate", j), GS[:, j % 2, :], ACT.Silu)
                    swish(2 * g + 2)
                    swish(2 * g + 3)
            norm.next_squares(act, lambda k: wait_read(act, ("outb", 3, k)))

        @block.vector
        def _(dve):
            v = nc.vector
            sums = [0]

            def next_level(instruction, of=None):
                instruction.then_inc(level, 1)
                sums[0] += 1
                dve.wait_ge(level, sums[0])

            def value(j):
                wait_result(dve, ("val", j))
                wait_read(dve, ("glu", j))
                if j:
                    dve.wait_ge(tails_turned, j)
                    dve.wait_ge(cv, TAPS * j)
                v.tensor_tensor(parts(V[:, HC:HC + TP]), bank(("val", j)), parts(SG[:, :]),
                                ALU.mult).then_inc(freed(("val", j)), 1)
                wait_read(dve, ("val", j))
                v.tensor_copy(VS[:, :, HC:HC + TS], V[:, HC + T:HC + TA].rearrange("p (b t) -> p b t", b=NB)).then_inc(vs_new, 1)

            def conv(j, first, last):
                if first == 0:
                    dve.wait_ge(hist_copied, 2 * j + 2)
                    dve.wait_ge(vs_new, j + 1)
                    if j >= 2:
                        dve.wait_ge(stored[j % 2], 16 * (j // 2))
                        dve.wait_ge(stats, 3 * (j - 1))
                outs = (CB[:, j % 2, 0:T], CB[:, j % 2, T:TA].rearrange("p (b t) -> p b t", b=NB))
                for n in range(first, last):
                    ins = (V[:, n:n + T], VS[:, :, n:n + TS])
                    tap = c.prm[:, j, ROW_CONV_W + n:ROW_CONV_W + n + 1]
                    for i in range(2):
                        if n == 0:
                            v.tensor_scalar(outs[i], ins[i], tap, c.prm[:, j, ROW_CONV_B:ROW_CONV_B + 1],
                                            ALU.mult, ALU.add).then_inc(cv, 1)
                        else:
                            dve.wait_ge(cv, TAPS * j + 2 * (n - 1) + i + 1)
                            v.scalar_tensor_tensor(outs[i], ins[i], tap, outs[i], ALU.mult, ALU.add).then_inc(cv, 1)

            def add_stats(j):
                dve.wait_ge(cv, TAPS * (j + 1))
                C = CB[:, j % 2, :]
                if j == 0:
                    v.tensor_copy(S1[:, :], C).then_inc(stats, 1)
                    dve.wait_ge(squared, 1)
                    v.tensor_copy(PT[:, 0:1], PT[:, TA:TA + 1]).then_inc(stats, 2)
                else:
                    dve.wait_ge(stats, 3 * j)
                    v.tensor_tensor(S1[:, :], S1[:, :], C, ALU.add).then_inc(stats, 1)
                    dve.wait_ge(squared, j + 1)
                    v.tensor_tensor(S2[:, :], S2[:, :], PT[:, :], ALU.add).then_inc(stats, 2)

            def pooling(j):
                w = 2 << j // 2
                wait_read(dve, ("ain", j))
                dve.wait_ge(hist_copied, 2 * j + 2)
                v.tensor_copy(AS[:, :, HPOOL:HPOOL + TS], A[:, HPOOL + T:HPOOL + TA].rearrange("p (b t) -> p b t", b=NB)
                              ).then_inc(as_new, 1)
                n = HPOOL + T
                next_level(v.tensor_tensor(PT[:, 0:n - 1], A[:, 0:n - 1], A[:, 1:n], ALU.add))
                dve.wait_ge(as_new, j + 1)
                dve.wait_ge(vs_new, j + 1)
                m = HPOOL + TS
                next_level(v.tensor_tensor(AT[:, :, 0:m - 1], AS[:, :, 0:m - 1], AS[:, :, 1:m], ALU.add))
                n, m, s = n - 1, m - 1, 2
                while s < w:
                    next_level(v.tensor_tensor(PT[:, 0:n - s], PT[:, 0:n - s], PT[:, s:n], ALU.add))
                    next_level(v.tensor_tensor(AT[:, :, 0:m - s], AT[:, :, 0:m - s], AT[:, :, s:m], ALU.add))
                    n, m, s = n - s, m - s, 2 * s
                for t in range(w - 1):
                    i = 16 - w + t
                    v.scalar_tensor_tensor(PT[:, t:t + 1], PT[:, i:i + 1], 1.0 / (t + 1), A[:, HPOOL + t:HPOOL + t + 1],
                                           ALU.mult, ALU.subtract).then_inc(level, 1)
                    sums[0] += 1
                dve.wait_ge(level, sums[0])
                next_level(v.scalar_tensor_tensor(PT[:, w - 1:T], PT[:, 15:16 - w + T], 1.0 / w, A[:, HPOOL + w - 1:HPOOL + T],
                                                  ALU.mult, ALU.subtract))
                v.scalar_tensor_tensor(PT[:, T:TA].rearrange("p (b t) -> p b t", b=NB), AT[:, :, 16 - w:16 - w + TS], 1.0 / w,
                                       AS[:, :, HPOOL:HPOOL + TS], ALU.mult, ALU.subtract).then_inc(m_done, 1)

            def pooled_low(j):
                dve.wait_ge(m_hi, j + 1)
                v.tensor_tensor(Ml[:, j % 2, :], PT[:, :], Mh[:, j % 2, :].bitcast(F32), ALU.subtract).then_inc(m_lo, 1)

            def ya(j):
                wait_result(dve, ("pool", j))
                wait_read(dve, ("agate", j))
                dve.wait_ge(m_lo, 2 * (j // 2) + 2)
                if j % 2:
                    dve.wait_ge(y_lo, j)
                v.scalar_tensor_tensor(parts(PT[:, :]), bank(("pool", j)), c.prm[:, j, ROW_POOL:ROW_POOL + 1],
                                       parts(GS[:, j % 2, :]), ALU.mult, ALU.mult).then_inc(freed(("pool", j)), 1)

            def y_low(j, n):
                dve.wait_ge(y_hi, n + 1)
                v.tensor_tensor(c.Yl[:, j % 2, :], PT[:, :], c.Yh[:, j % 2, :].bitcast(F32), ALU.subtract).then_inc(y_lo, 1)

            def add(kind, g, k):
                tile = (kind, g, k)
                wait_result(dve, tile)
                v.tensor_tensor(parts(c.X[:, k, :]), bank(tile), parts(c.X[:, k, :]), ALU.add).then_inc(freed(tile), 1)

            norm.vector(dve, ROW_MIX)
            dve.wait_ge(norm.lo, KD)
            v.memset(V[:, 0:HC], 0.0).then_inc(init, 1)
            v.memset(A[:, 0:HPOOL], 0.0).then_inc(init, 1)
            v.memset(CB[:, :, TA:TP], 0.0).then_inc(init, 1)
            v.memset(PT[:, TA:TP], 0.0).then_inc(init, 1)
            dve.wait_ge(init, 4)
            for g in range(4):
                for e in range(2):
                    j = 2 * g + e
                    value(j)
                    conv(j, 0, 8)
                    at = 8
                    pooling(j)
                    conv(j, at, at + 2)
                    at += 2
                    pooled_low(j)
                    dve.wait_ge(m_lo, j + 1)
                    if e == 0 and g:
                        for k in range(KD):
                            add("outa", g - 1, k)
                            conv(j, at, at + 1 + k % 2)
                            at += 1 + k % 2
                    if e == 1:
                        conv(j, at, 13)
                        ya(j - 1)
                        conv(j, 13, 15)
                        y_low(j - 1, j - 1)
                        dve.wait_ge(y_lo, j)
                        ya(j)
                        conv(j, 15, 17)
                        y_low(j, j)
                        dve.wait_ge(y_lo, j + 1)
                        at = 17
                    conv(j, at, CONV)
                    add_stats(j)
            wait_read(dve, ("sum", 0))
            dve.wait_ge(stats, 3 * KD)
            v.tensor_tensor(PT[:, :], SG[:, :], SG[:, :], ALU.mult).then_inc(ln_sq, 1)
            dve.wait_ge(ln_sq, 1)
            dve.wait_ge(ln_sum, 2)
            dve.wait_ge(tails_turned, KD)
            dve.wait_ge(cv, TAPS * KD)
            v.scalar_tensor_tensor(parts(V[:, 0:TP]), bank(("sum", 1)), 1.0 / WB, parts(PT[:, :]), ALU.mult,
                                   ALU.subtract).then_inc(freed(("sum", 1)), 1)
            wait_read(dve, ("sum", 1))
            v.tensor_scalar(V[:, 0:TP], V[:, 0:TP], 0.0, None, ALU.max).then_inc(ln_var, 1)
            for k in range(3):
                add("outa", 3, k)
            dve.wait_ge(ln_std, 1)
            v.reciprocal(V[:, 0:TP], V[:, 0:TP]).then_inc(ln_r, 1)
            dve.wait_ge(ln_r, 1)

            def normalise(j):
                dve.wait_ge(c_in[j % 2], 16 * (j // 2 + 1))
                v.tensor_tensor(CB[:, j % 2, :], CB[:, j % 2, :], SG[:, :], ALU.subtract).then_inc(centred, 1)
                dve.wait_ge(centred, j + 1)
                v.tensor_tensor(CB[:, j % 2, :], CB[:, j % 2, :], V[:, 0:TP], ALU.mult).then_inc(ln_x, 1)

            for k in range(3, 6):
                add("outa", 3, k)
            normalise(0)
            normalise(1)
            for k in range(6, KD):
                add("outa", 3, k)
            for g in range(4):
                for j in (2 * g, 2 * g + 1):
                    dve.wait_ge(ln_y, j + 1)
                    wait_read(dve, ("bgate", j))
                    if j:
                        dve.wait_ge(y_lo, KD + j)
                    v.tensor_tensor(PT[:, :], CB[:, j % 2, :], GS[:, j % 2, :], ALU.mult).then_inc(yb, 1)
                    y_low(j, KD + j)
                if g < 3:
                    normalise(2 * g + 2)
                    normalise(2 * g + 3)
                for k in range(KD):
                    if g == 0 and k == 0:
                        wait_read(dve, ("outa", 3, KD - 1))
                    add("outb", g, k)


def block_cross(c, layer):
    nc, r = c.nc, c.dram
    c.at = c.region
    name = f"a{layer}"
    TILES, HALVES, UNITS = 12, 32, 16
    NT = T // P
    S_TURN = 5
    w = {n: r[f"w_{n}"][layer] for n in "qkvo"}
    memory = r["mem_prompt"][0].rearrange("(a p) d -> p a d", p=P)
    with ExitStack() as ctx:
        sem = semaphores(c, ctx, f"{name}_")
        norm = Norm(c, sem)
        after_norm = c.at
        c.at = c.region
        Q = lay(c, f"{name}_Q", [P, 2, TP])
        PT = lay(c, f"{name}_PT", [P, 2, T])
        E = lay(c, f"{name}_E", [P, 2, MEM])
        c.at = max(c.at, after_norm)
        KTS = lay(c, f"{name}_KTS", [P, 2, 2 * MEM])
        QM = lay(c, f"{name}_QM", [P, 2, NB * 72])
        end_of_rows = c.at
        c.at -= 4096 + 2 * NB * 72 * 4
        MN = lay(c, f"{name}_MN", [P, 2, D])
        c.at = end_of_rows
        MTh = lay(c, f"{name}_MTh", [P, KD, MEM], F32R)
        MTl = lay(c, f"{name}_MTl", [P, KD, MEM], F32R)
        KN = lay(c, f"{name}_KN", [P, 2, HD])
        VN = lay(c, f"{name}_VN", [P, 2, HD])
        KT = lay(c, f"{name}_KT", [P, 2, MEM])
        KV = lay(c, f"{name}_KV", [P, NB, 2 * HD])
        PM = QM
        ES = KTS[0:NS, 0, 0:MEM]
        OS = KTS[0:NS, 1, 0:MEM]
        st = lay(c, f"{name}_st", [P, 16])
        NM, SUM, MS = st[:, 0:2], st[:, 2:4], st[:, 4:6]
        NMS, SUMS = st[0:NS, 6:7], st[0:NS, 7:8]
        G = Gemm(c, sem)
        mem_in, mem_sq, mem_std, mem_r, mem_n = sem("mem_in"), sem("mem_sq"), sem("mem_std"), sem("mem_r"), sem("mem_n")
        mem_turned, mt_hi, mt_lo, init = sem("mem_turned"), sem("mt_hi"), sem("mt_lo"), sem("init")
        kv_in = [sem(f"kv_in{i}") for i in range(NB)]
        kt_turned, kt_copied, k_stored, v_stored, qm_set = sem("kt_turned"), sem("kt_copied"), sem("k_stored"), sem("v_stored"), sem("qm_set")
        scored, maxed, exped, inverted, weighed = sem("scored"), sem("maxed"), sem("exped"), sem("inverted"), sem("weighed")
        p_turned, p_copied = sem("p_turned"), sem("p_copied")
        ks_turned, ks_copied, s_scored = sem("ks_turned"), sem("ks_copied"), sem("s_scored")
        s_maxed, s_exped, s_inverted, s_weighed = sem("s_maxed"), sem("s_exped"), sem("s_inverted"), sem("s_weighed")
        s_turned, s_copied, v_used = sem("s_turned"), sem("s_copied"), sem("v_used")
        so_copied, o_done = sem("so_copied"), sem("o_done")
        y_hi, y_lo = sem("y_hi"), sem("y_lo")
        block = ctx.enter_context(nc.Block())

        FIRST, LATER = ("k", "v", "q0", "q1"), ("q0", "k", "q1", "v")
        TILE_UNITS = {"q0": 2, "q1": 2, "k": 4, "v": 4}
        GROUP_FIRST = {"k": (0, 0), "q0": (0, 1), "v": (1, 0), "q1": (1, 1)}
        GROUP_LATER = {"q0": (0, 0), "q1": (0, 1), "k": (1, 0), "v": (1, 1)}

        def unit(n, first):
            order = FIRST if first else LATER
            return 12 + n // 2 if n in range(KD) else sum(TILE_UNITS[m] for m in order[:order.index(n)])

        def tile_group(n, first):
            return (n % 2, 2 + n // 2) if n in range(KD) else (GROUP_FIRST if first else GROUP_LATER)[n]

        def memory_banks(n, first):
            if n == "v" and not first:
                return c.PS[:, 5, :].rearrange("p (a n) -> p a n", a=2)
            return group(c, tile_group(n, first)[0])[:, 0:2, 0:HD]

        def wait_result(e, h, n, first):
            if n in range(KD):
                e.wait_ge(G.half, h * HALVES + 25 + n)
            elif first and n == "q0":
                e.wait_ge(G.half, 2 * unit(n, first) + 6)
            else:
                e.wait_ge(G.half, h * HALVES + 2 * (unit(n, first) + TILE_UNITS[n]))

        def wait_read(e, h, n, first=False):
            b, i = tile_group(n, first)
            e.wait_ge(G.freed[b], h * (TILES // 2) + i + 1)

        def heads(e, body):
            body(0, True)
            with e.Fori(1, NH) as h:
                body(h, False)

        @block.sync
        def _(sp):
            sp.dma_start(MN[:, :, :], memory).then_inc(mem_in, 16)

            def head(h, first):
                def rows_256(m):
                    v = w[m].rearrange("(q k p) n -> q p k n", k=2, p=P)
                    return [v[q, :, :, bass.ds(h * HD, HD)] for q in range(4)]

                if first:
                    srcs = rows_256("k") + rows_256("v") + first_units(w["q"], 0, P)
                else:
                    srcs = in_units(w["q"], h * HD) + rows_256("k") + in_units(w["q"], h * HD + P) + rows_256("v")
                for u, src in enumerate(srcs):
                    G.load(sp, h * UNITS + u, u, src, wait=not first or u >= RAW)

                def cached(b, which):
                    if which == "v":
                        sp.wait_ge(ks_turned, h * NB + b + 1)
                    elif not first:
                        sp.wait_ge(v_used, (h - 1) * NB + b + 1)
                    src = r[f"cache_mem_{which}"][layer, b].rearrange("(a p) h d -> p a h d", p=P)[:, :, bass.ds(h, 1), :]
                    sp.dma_start(KV[:, b, :].rearrange("p (a o d) -> p a o d", a=2, o=1), src).then_inc(kv_in[b], 16)

                for b in range(NB):
                    cached(b, "k")
                for q, src in enumerate(out_units(w["o"], h * HD)):
                    G.load(sp, h * UNITS + 12 + q, q, src)
                for b in range(NB):
                    cached(b, "v")

            heads(sp, head)
            sp.wait_ge(k_stored, 16 * NH)
            sp.wait_ge(v_stored, 16 * NH)

        @block.gpsimd
        def _(pool):
            G.split_all(pool, UNITS * NH)
            norm.next_sums(pool)

        MB = ((0, 1), (2, 6))

        @block.tensor
        def _(pe):
            norm.tensor(pe)
            pe.wait_ge(mem_n, 2)
            for a in range(2):
                for kh in range(2):
                    for k in range(4):
                        mm = pe.transpose(c.PS[:, MB[a][kh], k * P:(k + 1) * P],
                                          MN[:, a, (4 * kh + k) * P:(4 * kh + k + 1) * P], c.ident[:, :])
                    mm.then_inc(mem_turned, 1)

            def memory_tile(h, first, n, chunks=range(KD)):
                out = memory_banks(n, first)
                shared = n == "v" and not first
                for k in chunks:
                    u = unit(n, first) + k // 2
                    if k % 2 == 0:
                        pe.wait_ge(G.w_split, h * UNITS + u + 1)
                    s = u % SPLIT
                    cols = slice((k % 2) * HD, (k % 2 + 1) * HD)
                    for i, (m, x) in enumerate(((MTh, c.Wh), (MTh, c.Wl), (MTl, c.Wh))):
                        for a in range(2):
                            mm = pe.matmul(out[:, a, :], m[:, k, a * P:(a + 1) * P], x[:, s, cols],
                                           start=k == 0 and i == 0 and (a == 0 or not shared),
                                           stop=k == KD - 1 and i == 2 and (a == 1 or not shared))
                    mm.then_inc(G.half, 1)

            def turn_k(h, first):
                wait_read(pe, h, "k", first)
                if not first:
                    pe.wait_ge(p_copied, h * NT)
                for d in range(2):
                    for a in range(2):
                        mm = pe.transpose(c.PS[:, 7, d * MEM + a * P:d * MEM + (a + 1) * P],
                                          KN[:, a, d * P:(d + 1) * P], c.ident[:, :])
                mm.then_inc(kt_turned, 1)

            def sample_k(h, b):
                pe.wait_ge(kv_in[b], h * 32 + 16)
                if b >= 2:
                    pe.wait_ge(ks_copied, h * NB + b - 1)
                for a in range(2):
                    for d in range(2):
                        mm = pe.transpose(c.PS[:, 3 + b % 2, d * MEM + a * P:d * MEM + (a + 1) * P],
                                          KV[:, b, a * HD + d * P:a * HD + (d + 1) * P], c.ident[:, :])
                mm.then_inc(ks_turned, 1)

            def sample_scores(h, b):
                pe.wait_ge(ks_copied, h * NB + b + 1)
                if b == 0:
                    pe.wait_ge(qm_set, h * 2 + 2)
                for d in range(2):
                    mm = pe.matmul(c.PS[0:NS, 2, 0:MEM], QM[:, d, NS * b:NS * (b + 1)], KTS[:, b % 2, d * MEM:(d + 1) * MEM],
                                   start=b == 0 and d == 0, stop=b == NB - 1 and d == 1)
                mm.then_inc(s_scored, 1)

            def scores(h, t):
                if t >= 2:
                    pe.wait_ge(exped, h * NT + t - 1)
                for d in range(2):
                    mm = pe.matmul(c.PS[:, t % 2, 0:MEM], Q[:, d, t * P:(t + 1) * P], KT[:, d, :], start=d == 0, stop=d == 1)
                mm.then_inc(scored, 1)

            def turn(h, t):
                pe.wait_ge(weighed, h * NT + t + 1)
                if t >= 2:
                    pe.wait_ge(p_copied, h * NT + t - 1)
                for a in range(2):
                    mm = pe.transpose(c.PS[:, 6 + t % 2, a * P:(a + 1) * P], E[:, t % 2, a * P:(a + 1) * P], c.ident[:, :])
                mm.then_inc(p_turned, 1)

            def turn_samples(h):
                for a in range(2):
                    mm = pe.transpose(c.PS[:, 4, a * NS:(a + 1) * NS], ES[:, a * P:(a + 1) * P], c.ident[0:NS, 0:NS])
                mm.then_inc(s_turned, 1)

            def sample_o(h, b):
                pe.wait_ge(kv_in[b], h * 32 + 32)
                for a in range(2):
                    mm = pe.matmul(c.PS[0:NS, 3, 0:HD], PM[:, a, NS * b:NS * (b + 1)], KV[:, b, a * HD:(a + 1) * HD],
                                   start=b == 0 and a == 0, stop=b == NB - 1 and a == 1)
                mm.then_inc(v_used, 1)

            def turned_o(h, d):
                for q in range(3):
                    lo, hi = q * PART, min((q + 1) * PART, T)
                    if d == 0 and q == 2:
                        pe.wait_ge(so_copied, h + 1)
                    for a in range(2):
                        pe.matmul(group(c, d)[:, q, 0:hi - lo], VN[:, a, d * P:(d + 1) * P], PT[:, a, lo:hi],
                                  start=a == 0, stop=a == 1)
                pe.matmul(group(c, d)[:, 2, T - 2 * PART:PART], OS[:, d * P:(d + 1) * P], c.ident[0:NS, 0:NS + 4],
                          start=True, stop=True).then_inc(o_done, 1)

            def head(h, first):
                if first:
                    pe.wait_ge(mt_lo, 4)
                    memory_tile(h, first, "k")
                    pe.wait_ge(norm.rstd, 2)
                    memory_tile(h, first, "v")
                    wait_read(pe, h, "k", first)
                    wait_read(pe, h, "v", first)
                    G.first_tiles(pe, norm.lo, unit("q0", first))
                    turn_k(h, first)
                else:
                    wait_read(pe, h - 1, KD - 2)
                    G.in_tile(pe, h * UNITS, 0, 0, None)
                    wait_read(pe, h - 1, KD - 1)
                    memory_tile(h, first, "k")
                    wait_read(pe, h, "q0")
                    G.in_tile(pe, h * UNITS + unit("q1", first), unit("q1", first), 0, None)
                    turn_k(h, first)
                    memory_tile(h, first, "v", range(KD // 2))
                wait_read(pe, h, "q0", first)
                wait_read(pe, h, "q1", first)
                pe.wait_ge(kt_copied, h + 1)
                scores(h, 0)
                scores(h, 1)
                if first:
                    wait_read(pe, h, "v", first)
                sample_k(h, 0)
                sample_k(h, 1)
                for t in range(NT):
                    if t < NB // 2:
                        for b in (2 * t, 2 * t + 1):
                            sample_scores(h, b)
                            if b + 2 < NB:
                                sample_k(h, b + 2)
                    if not first and t >= NT - KD // 2:
                        memory_tile(h, first, "v", [t - NT + KD])
                    if t == S_TURN:
                        pe.wait_ge(s_weighed, h + 1)
                    turn(h, t)
                    if t + 2 < NT:
                        scores(h, t + 2)
                    if t == S_TURN:
                        turn_samples(h)
                    if t == NT - 2:
                        pe.wait_ge(s_copied, h * 2 + 2)
                        for b in range(NB // 2):
                            sample_o(h, b)
                for b in range(NB // 2, NB):
                    sample_o(h, b)
                pe.wait_ge(p_copied, h * NT + NT)
                wait_read(pe, h, "v", first)
                turned_o(h, 0)
                turned_o(h, 1)
                for k in range(KD):
                    if k % 2 == 0:
                        pe.wait_ge(G.w_split, h * UNITS + 12 + k // 2 + 1)
                    if k == 0:
                        pe.wait_ge(y_lo, h * 2 + 1)
                    elif k == 1:
                        pe.wait_ge(y_lo, h * 2 + 2)
                    else:
                        wait_read(pe, h, k - 2)
                    G.pair_tile(pe, k // 2, k % 2, k % 2, None, c.Yh, c.Yl,
                                second=(y_lo, h * 2 + 2) if k == 0 else None)

            heads(pe, head)

        @block.scalar
        def _(act):
            s = nc.scalar
            norm.scalar_std(act)
            act.wait_ge(mem_in, 16)
            for a in range(2):
                s.activation(MTh[:, 4 * a:4 * a + 4, :], MN[:, a, :].rearrange("p (k n) -> p k n", k=4), ACT.Square,
                             accum_out=MS[:, a:a + 1]).then_inc(mem_sq, 1)
            act.wait_ge(mem_sq, 2)
            s.activation(MS, MS, ACT.Sqrt, bias=c.eps[:, 0:1], scale=1.0 / D).then_inc(mem_std, 1)
            for n, (a, kh) in enumerate(((0, 0), (0, 1), (1, 0), (1, 1))):
                act.wait_ge(mem_turned, n + 1)
                for k in range(4):
                    k8 = 4 * kh + k
                    mm = s.activation(MTh[:, k8, a * P:(a + 1) * P], c.PS[:, MB[a][kh], k * P:(k + 1) * P], ACT.Copy,
                                      scale=c.prm[:, k8, ROW_MEM + layer:ROW_MEM + layer + 1])
                mm.then_inc(mt_hi, 1)
            def keep(h, first, n):
                rows, stored, out = {"k": (KN, k_stored, r["new_mem_k"]), "v": (VN, v_stored, r["new_mem_v"])}[n]
                wait_result(act, h, n, first)
                if not first:
                    act.wait_ge(stored, h * 16)
                    if n == "k":
                        act.wait_ge(kt_turned, h)
                    else:
                        act.wait_ge(o_done, h * 2)
                b = tile_group(n, first)[0]
                s.activation(rows[:, :, :], memory_banks(n, first), ACT.Copy).then_inc(G.freed[b], 1)
                wait_read(act, h, n, first)
                dst = out[layer, 0].rearrange("(a p) h d -> p a h d", p=P)[:, :, bass.ds(h, 1), :]
                act.dma_start(dst, rows[:, :, :].rearrange("p a (o d) -> p a o d", o=1)).then_inc(stored, 16)

            def head(h, first):
                for n in FIRST if first else LATER[:3]:
                    if n in ("k", "v"):
                        if first:
                            norm.scalar_split(act, *((0, 3) if n == "k" else (3, 5)))
                        keep(h, first, n)
                        if first and n == "v":
                            norm.scalar_split(act, 5)
                    else:
                        wait_result(act, h, n, first)
                        if not first and n == "q0":
                            act.wait_ge(scored, h * NT)
                        b = tile_group(n, first)[0]
                        s.activation(parts(Q[:, int(n[1]), :]), group(c, b)[:, :, 0:PART], ACT.Copy,
                                     scale=HD ** -0.5).then_inc(G.freed[b], 1)
                    if n == "q1":
                        act.wait_ge(kt_turned, h + 1)
                        s.activation(KT[:, :, :], c.PS[:, 7, :].rearrange("p (d m) -> p d m", d=2), ACT.Copy).then_inc(kt_copied, 1)

                def copy_turned(t):
                    act.wait_ge(p_turned, h * NT + t + 1)
                    s.activation(PT[:, :, t * P:(t + 1) * P], c.PS[:, 6 + t % 2, 0:2 * P].rearrange("p (a n) -> p a n", a=2),
                                 ACT.Copy).then_inc(p_copied, 1)

                for t in range(NT):
                    if t >= 2 or not first:
                        act.wait_ge(p_turned, h * NT + t - 1)
                    act.wait_ge(maxed, h * NT + t + 1)
                    s.activation(E[:, t % 2, :], c.PS[:, t % 2, 0:MEM], ACT.Exp, bias=NM[:, t % 2:t % 2 + 1],
                                 accum_out=SUM[:, t % 2:t % 2 + 1]).then_inc(exped, 1)
                    if t >= 1:
                        copy_turned(t - 1)
                    if t == S_TURN + 1:
                        act.wait_ge(s_turned, h + 1)
                        for a in range(2):
                            s.activation(PM[:, a, :].rearrange("p (b n) -> p b n", b=NB)[:, :, 0:TS],
                                         c.PS[:, 4, a * NS:(a + 1) * NS].rearrange("p (b t) -> p b t", b=NB),
                                         ACT.Copy).then_inc(s_copied, 1)
                    if t == S_TURN - 1:
                        act.wait_ge(s_maxed, h + 1)
                        s.activation(ES, c.PS[0:NS, 2, 0:MEM], ACT.Exp, bias=NMS, accum_out=SUMS).then_inc(s_exped, 1)
                copy_turned(NT - 1)
                if not first:
                    keep(h, first, "v")
                act.wait_ge(v_used, h * NB + NB)
                s.activation(OS, c.PS[0:NS, 3, 0:MEM], ACT.Copy).then_inc(so_copied, 1)
                for d in range(2):
                    act.wait_ge(o_done, h * 2 + d + 1)
                    s.activation(parts(c.Yh[:, d, :]), group(c, d)[:, :, 0:PART], ACT.Copy).then_inc(y_hi, 1)

            heads(act, head)
            norm.next_squares(act, lambda k: wait_read(act, NH - 1, k))

        @block.vector
        def _(dve):
            v = nc.vector
            norm.vector_rstd(dve)
            dve.wait_ge(mem_std, 1)
            v.reciprocal(MS, MS).then_inc(mem_r, 1)
            dve.wait_ge(mem_r, 1)
            for a in range(2):
                v.tensor_scalar(MN[:, a, :], MN[:, a, :], MS[:, a:a + 1], None, ALU.mult).then_inc(mem_n, 1)
            for n, (a, kh) in enumerate(((0, 0), (0, 1), (1, 0), (1, 1))):
                dve.wait_ge(mt_hi, n + 1)
                for k in range(4):
                    k8 = 4 * kh + k
                    mm = v.scalar_tensor_tensor(MTl[:, k8, a * P:(a + 1) * P], c.PS[:, MB[a][kh], k * P:(k + 1) * P],
                                                c.prm[:, k8, ROW_MEM + layer:ROW_MEM + layer + 1],
                                                MTh[:, k8, a * P:(a + 1) * P].bitcast(F32), ALU.mult, ALU.subtract)
                mm.then_inc(mt_lo, 1)
            dve.wait_ge(mem_turned, 4)
            v.memset(QM[:, :, :], 0.0).then_inc(init, 1)
            norm.vector_split(dve, ROW_X + layer)
            dve.wait_ge(init, 1)

            def head(h, first):
                if not first:
                    dve.wait_ge(v_used, h * NB)
                for d in range(2):
                    wait_read(dve, h, f"q{d}", first)
                    v.tensor_copy(QM[:, d, :].rearrange("p (b n) -> p b n", b=NB)[:, :, 0:TS],
                                  Q[:, d, T:TA].rearrange("p (b t) -> p b t", b=NB)).then_inc(qm_set, 1)

                def maximum(t):
                    dve.wait_ge(scored, h * NT + t + 1)
                    v.tensor_reduce(NM[:, t % 2:t % 2 + 1], c.PS[:, t % 2, 0:MEM], AX_X, ALU.max, negate=True).then_inc(maxed, 1)

                def sample_k(b):
                    dve.wait_ge(ks_turned, h * NB + b + 1)
                    if b >= 2 or not first:
                        dve.wait_ge(s_scored, h * NB + b - 1)
                    v.tensor_copy(KTS[:, b % 2, :], c.PS[:, 3 + b % 2, :]).then_inc(ks_copied, 1)

                maximum(0)
                if not first:
                    dve.wait_ge(o_done, h * 2)
                sample_k(0)
                maximum(1)
                sample_k(1)
                for t in range(NT):
                    i = t % 2
                    dve.wait_ge(exped, h * NT + t + 1)
                    v.reciprocal(SUM[:, i:i + 1], SUM[:, i:i + 1]).then_inc(inverted, 1)
                    dve.wait_ge(inverted, h * NT + t + 1)
                    v.tensor_scalar(E[:, i, :], E[:, i, :], SUM[:, i:i + 1], None, ALU.mult).then_inc(weighed, 1)
                    if 2 * t + 2 < NB:
                        sample_k(2 * t + 2)
                        sample_k(2 * t + 3)
                    if t + 2 < NT:
                        maximum(t + 2)
                    if t == S_TURN - 2:
                        dve.wait_ge(s_scored, h * NB + NB)
                        v.tensor_reduce(NMS, c.PS[0:NS, 2, 0:MEM], AX_X, ALU.max, negate=True).then_inc(s_maxed, 1)
                    if t == S_TURN - 1:
                        dve.wait_ge(s_exped, h + 1)
                        v.reciprocal(SUMS, SUMS).then_inc(s_inverted, 1)
                        dve.wait_ge(s_inverted, h + 1)
                        v.tensor_scalar(ES, ES, SUMS, None, ALU.mult).then_inc(s_weighed, 1)
                for d in range(2):
                    dve.wait_ge(y_hi, h * 2 + d + 1)
                    v.tensor_tensor(parts(c.Yl[:, d, :]), group(c, d)[:, :, 0:PART], parts(c.Yh[:, d, :].bitcast(F32)),
                                    ALU.subtract).then_inc(y_lo, 1)
                for k in range(KD):
                    wait_result(dve, h, k, first)
                    if not first:
                        wait_read(dve, h - 1, k)
                    v.tensor_tensor(parts(c.X[:, k, :]), group(c, k % 2)[:, :, 0:PART], parts(c.X[:, k, :]),
                                    ALU.add).then_inc(G.freed[k % 2], 1)

            heads(dve, head)


def block_odd(c, name):
    nc, r = c.nc, c.dram
    c.at = c.region
    PAIRS = WC // 256
    w_in, w_out = r["w_in_odd"][0], r["w_out_odd"][0]
    hist_rows = r["state_short"][0].rearrange("b t c -> (b t) c")
    with ExitStack() as ctx:
        sem = semaphores(c, ctx, f"{name}_")
        norm = Norm(c, sem)
        XV = lay(c, f"{name}_XV", [P, TP])
        U = lay(c, f"{name}_U", [P, HS + TP])
        US = lay(c, f"{name}_US", [P, NB, HS + TS])
        CV = lay(c, f"{name}_CV", [P, 2, TP])
        GS = lay(c, f"{name}_GS", [P, TP])
        SW = lay(c, f"{name}_SW", [P, WC // P, 3])
        TL = lay(c, f"{name}_TL", [P, NB * HS])
        SN = lay(c, f"{name}_SN", [P, P])
        OS = lay(c, f"{name}_OS", [P, 2, P])
        G = Gemm(c, sem)
        hist_in, hist_turned, hist_copied = sem("hist_in"), sem("hist_turned"), sem("hist_copied")
        tail_copied = sem("tail_copied")
        u_turned, rows_copied, rows_stored = sem("u_turned"), sem("rows_copied"), sem("rows_stored")
        init, us_new, cv, y_done, y_hi, y_lo = sem("init"), sem("us_new"), sem("cv"), sem("y_done"), sem("y_hi"), sem("y_lo")
        block = ctx.enter_context(nc.Block())

        def chunk(g, odd):
            if isinstance(g, int) and g == 0:
                return odd, 8 * odd, 4 * odd
            return g * 2 + odd, g * 20 + (8 if odd else -4), g * 16 + (4 if odd else -8)

        def projection(g, last=False):
            return (g * 20 + 24, g * 16 + 12) if not last else (g * 20 + 16, g * 16 + 8)

        def tile_done(u, i):
            if isinstance(u, int) and u == 0 and i == 0:
                return 6
            return u * 2 + 4 * (i + 1)

        def read(t, i):
            return t_half(t) + i // 2 + 1

        def t_half(t):
            return t // 2

        @block.sync
        def _(sp):
            def load_chunk(g, odd):
                j, u, t = chunk(g, odd)
                if odd or not isinstance(g, int):
                    sp.wait_ge(hist_turned, j)
                sp.dma_start(SN[0:NB * HS, :], hist_rows[:, bass.ds(j * P, P)]).then_inc(hist_in, 16)
                first = isinstance(g, int) and not odd
                cols = [j * P + part * WC for part in (2, 1, 3, 0)]
                srcs = first_units(w_in, cols[0], cols[1]) if first else in_units(w_in, cols[0]) + in_units(w_in, cols[1])
                for n, src in enumerate(srcs + in_units(w_in, cols[2]) + in_units(w_in, cols[3])):
                    G.load(sp, u + n, n, src, wait=not first or n >= RAW)

            def load_out(g, last=False):
                u, t = projection(g, last)
                for q, src in enumerate(out_units(w_out, g * 256)):
                    G.load(sp, u + q, q, src)

            load_chunk(0, 0)
            load_chunk(0, 1)
            with sp.Fori(1, PAIRS) as g:
                load_chunk(g, 0)
                load_out(g - 1)
                load_chunk(g, 1)
            load_out(PAIRS - 1, True)
            sp.wait_ge(rows_stored, 32 * 2 * PAIRS)

        @block.gpsimd
        def _(pool):
            G.split_all(pool, 20 * PAIRS)
            norm.next_sums(pool)

        @block.tensor
        def _(pe):
            def in_chunk(g, odd):
                j, u, t = chunk(g, odd)
                first = isinstance(g, int)
                pe.wait_ge(hist_in, (j + 1) * 16)
                if not first or odd:
                    pe.wait_ge(hist_copied, j)
                for i in range(4):
                    if first and not odd and i < 2:
                        if i == 0:
                            pe.wait_ge(norm.rstd, 2)
                            G.first_tiles(pe, norm.lo)
                    else:
                        G.in_tile(pe, u + 2 * i, 2 * i, i % 2, t_half(t) + i // 2)
                    if i == 0:
                        pe.transpose(c.PS[:, 6, 0:NB * HS], SN[0:NB * HS, :],
                                     c.ident[0:NB * HS, 0:NB * HS]).then_inc(hist_turned, 1)
                pe.wait_ge(us_new, j + 1)
                pe.wait_ge(tail_copied, j + 1)
                if not first or odd:
                    pe.wait_ge(rows_copied, j * 2)
                pe.transpose(c.PS[0:HS, 7, 0:P], U[:, T:HS + T], c.ident[:, :])
                pe.transpose(c.PS[0:NB * HS, 7, P:2 * P], TL[:, :], c.ident[:, :]).then_inc(u_turned, 1)

            def project(g, last=False):
                u, t = projection(g, last)
                pe.wait_ge(y_lo, g * 2 + 2)
                for k in range(KD):
                    if k % 2 == 0:
                        pe.wait_ge(G.w_split, u + k // 2 + 1)
                    G.pair_tile(pe, k // 2, k % 2, k % 2, t_half(t) + k // 2, c.Yh, c.Yl)

            norm.tensor(pe)
            in_chunk(0, 0)
            in_chunk(0, 1)
            with pe.Fori(1, PAIRS) as g:
                in_chunk(g, 0)
                project(g - 1)
                in_chunk(g, 1)
            project(PAIRS - 1, True)

        @block.scalar
        def _(act):
            def in_chunk(g, odd):
                j, u, t = chunk(g, odd)
                first = isinstance(g, int)
                again = odd or not first
                act.wait_ge(hist_turned, j + 1)
                if again:
                    act.wait_ge(cv, j * 6)
                nc.scalar.activation(US[:, :, 0:HS], c.PS[:, 6, 0:NB * HS].rearrange("p (b t) -> p b t", b=NB),
                                     ACT.Copy).then_inc(hist_copied, 1)
                act.wait_ge(G.half, tile_done(u, 0))
                if again:
                    act.wait_ge(y_done, j)
                nc.scalar.activation(parts(XV[:, :]), group(c, 0)[:, :, 0:PART], ACT.Copy).then_inc(G.freed[0], 1)
                act.wait_ge(G.half, tile_done(u, 2))
                nc.scalar.activation(parts(GS[:, :]), group(c, 0)[:, :, 0:PART], ACT.Silu).then_inc(G.freed[0], 1)
                act.wait_ge(us_new, j + 1)
                act.wait_ge(hist_copied, j + 1)
                nc.scalar.activation(TL[:, :].rearrange("p (b t) -> p b t", b=NB), US[:, :, TS:HS + TS],
                                     ACT.Copy).then_inc(tail_copied, 1)
                act.wait_ge(u_turned, j + 1)
                if again:
                    act.wait_ge(rows_stored, j * 32)
                nc.scalar.activation(OS[0:HS, 0, :], c.PS[0:HS, 7, 0:P], ACT.Copy).then_inc(rows_copied, 1)
                nc.scalar.activation(OS[0:NB * HS, 1, :], c.PS[0:NB * HS, 7, P:2 * P], ACT.Copy).then_inc(rows_copied, 1)
                act.wait_ge(rows_copied, j * 2 + 2)
                cols = bass.ds(j * P, P)
                act.dma_start(r["new_short_prompt"][0, 0, :, cols], OS[0:HS, 0, :]).then_inc(rows_stored, 16)
                act.dma_start(r["new_short_sample"][0].rearrange("b t c -> (b t) c")[:, cols],
                              OS[0:NB * HS, 1, :]).then_inc(rows_stored, 16)
                act.wait_ge(y_done, j + 1)
                if not first:
                    up, tp = projection(g - 1)
                    act.wait_ge(G.half, up * 2 + KD)
                nc.scalar.activation(c.Yh[:, odd, :], CV[:, odd, :], ACT.Copy).then_inc(y_hi, 1)

            norm.scalar(act)
            in_chunk(0, 0)
            in_chunk(0, 1)
            with act.Fori(1, PAIRS) as g:
                in_chunk(g, 0)
                in_chunk(g, 1)
            t_last = projection(PAIRS - 1, True)[1]
            norm.next_squares(act, lambda k: act.wait_ge(G.freed[k % 2], t_half(t_last) + k // 2 + 1))

        @block.vector
        def _(dve):
            v = nc.vector

            def in_chunk(g, odd):
                j, u, t = chunk(g, odd)
                first = isinstance(g, int)
                again = odd or not first
                dve.wait_ge(G.half, tile_done(u, 1))
                dve.wait_ge(G.freed[0], read(t, 0))
                if again:
                    dve.wait_ge(u_turned, j)
                    dve.wait_ge(cv, j * 6)
                v.tensor_tensor(parts(U[:, HS:HS + TP]), group(c, 1)[:, :, 0:PART], parts(XV[:, :]),
                                ALU.mult).then_inc(G.freed[1], 1)
                dve.wait_ge(G.freed[1], read(t, 1))
                v.tensor_copy(US[:, :, HS:HS + TS], U[:, HS + T:HS + TA].rearrange("p (b t) -> p b t", b=NB)).then_inc(us_new, 1)
                if not first:
                    dve.wait_ge(y_lo, j - 1)
                dve.wait_ge(us_new, j + 1)
                dve.wait_ge(hist_copied, j + 1)
                outs = (CV[:, odd, 0:T], CV[:, odd, T:TA].rearrange("p (b t) -> p b t", b=NB))
                for n in range(3):
                    ins = (U[:, n:n + T], US[:, :, n:n + TS])
                    tap = SW[:, bass.ds(j, 1), n]
                    for s in range(2):
                        if n == 0:
                            v.tensor_scalar(outs[s], ins[s], tap, None, ALU.mult).then_inc(cv, 1)
                        else:
                            dve.wait_ge(cv, j * 6 + 2 * (n - 1) + s + 1)
                            v.scalar_tensor_tensor(outs[s], ins[s], tap, outs[s], ALU.mult, ALU.add).then_inc(cv, 1)
                dve.wait_ge(cv, j * 6 + 6)
                dve.wait_ge(G.half, tile_done(u, 3))
                v.tensor_tensor(parts(CV[:, odd, :]), group(c, 1)[:, :, 0:PART], parts(CV[:, odd, :]),
                                ALU.mult).then_inc(G.freed[1], 1)
                dve.wait_ge(G.freed[1], read(t, 3))
                dve.wait_ge(G.freed[0], read(t, 2))
                v.tensor_tensor(CV[:, odd, :], CV[:, odd, :], GS[:, :], ALU.mult).then_inc(y_done, 1)

            def low(j, odd):
                dve.wait_ge(y_hi, j + 1)
                v.tensor_tensor(c.Yl[:, odd, :], CV[:, odd, :], c.Yh[:, odd, :].bitcast(F32),
                                ALU.subtract).then_inc(y_lo, 1)

            def add(g, last=False):
                u, t = projection(g, last)
                for k in range(KD):
                    dve.wait_ge(G.half, u * 2 + k + 1)
                    v.tensor_tensor(parts(c.X[:, k, :]), group(c, k % 2)[:, :, 0:PART], parts(c.X[:, k, :]),
                                    ALU.add).then_inc(G.freed[k % 2], 1)
                    dve.wait_ge(G.freed[k % 2], t_half(t) + k // 2 + 1)

            v.memset(U[:, 0:HS], 0.0).then_inc(init, 1)
            v.memset(CV[:, :, TA:TP], 0.0).then_inc(init, 1)
            for n in range(3):
                for h in range(2):
                    v.tensor_copy(SW[:, KD * h:KD * (h + 1), n], c.prm[:, :, ROW_SHORT + 2 * n + h]).then_inc(init, 1)
            norm.vector(dve, ROW_MIX + 1)
            dve.wait_ge(init, 8)
            in_chunk(0, 0)
            low(0, 0)
            in_chunk(0, 1)
            low(1, 1)
            with dve.Fori(1, PAIRS) as g:
                in_chunk(g, 0)
                add(g - 1)
                low(g * 2, 0)
                in_chunk(g, 1)
                low(g * 2 + 1, 1)
            add(PAIRS - 1, True)



def program(nc, dram):
    c = Core()
    c.nc, c.dram = nc, dram
    with ExitStack() as ctx:
        c.PS = ctx.enter_context(nc.psum_tensor("PS", [P, 8, 512], F32))
        place(c)
        block_load(c)
        block_even(c)
        block_cross(c, 0)
        block_odd(c, "odd")
        block_cross(c, 1)
        block_final(c)


_INS = ["x_prompt", "x_sample", "state_pool", "state_conv", "state_short", "cache_mem_k", "cache_mem_v", "mem_prompt",
        "norm_mix", "w_in_even", "pool_w", "pool_scale", "conv_w", "conv_b", "ln_g", "ln_b", "w_out_even",
        "w_in_odd", "short_w", "w_out_odd", "norm_x", "norm_mem", "w_q", "w_k", "w_v", "w_o", "final_norm"]
_OUTS = [("y_prompt", (1, T, D)), ("y_sample", (NB, TS, D)), ("new_pool_prompt", (1, 1, HPOOL, WB)),
         ("new_conv_prompt", (1, 1, HC, WB)), ("new_short_prompt", (1, 1, HS, WC)),
         ("new_mem_k", (2, 1, MEM, NH, HD)), ("new_mem_v", (2, 1, MEM, NH, HD)),
         ("new_pool_sample", (1, NB, HPOOL, WB)), ("new_conv_sample", (1, NB, HC, WB)), ("new_short_sample", (1, NB, HS, WC))]


def kernel(**inputs):
    import numpy as _np
    import concourse.bacc as _bacc
    from concourse import mybir as _mybir
    from concourse.bass_utils import run_bass_kernel_spmd as _run

    nc = _bacc.Bacc("TRN2", target_bir_lowering=False, num_devices=1)
    arrays, dram = {}, {}
    for name in _INS:
        a = _np.ascontiguousarray(inputs[name])
        arrays[f"in_{name}"] = a
        dram[name] = nc.dram_tensor(f"in_{name}", a.shape, _mybir.dt.from_np(a.dtype), kind="ExternalInput").ap()
    for name, shape in _OUTS:
        dram[name] = nc.dram_tensor(f"out_{name}", shape, _mybir.dt.float32, kind="ExternalOutput").ap()
    dram["conv_scratch"] = nc.dram_tensor("conv_scratch", (KD, P, TP), _mybir.dt.float32, kind="Internal").ap()
    program(nc, dram)
    r = _run(nc, [arrays], core_ids=[0])
    return tuple(r.results[0][f"out_{name}"] for name, _ in _OUTS)
```
